# Optimizing a Trainium2 kernel written in Bass

```python
import math
import jax, jax.numpy as jnp
from jax import lax
import numpy as np
import jax
import jax.numpy as jnp

D_MODEL = 1024
BATCH = 1
SEQ = 256
DEPTH = 2

N_META = 16
Q_BLOCK = 128
GROUP_HEAD_DIM = 64
D_MIX = D_MODEL
ATTN_HEADS = 8
ATTN_HEAD_DIM = 64
D_ATTN = ATTN_HEADS * ATTN_HEAD_DIM
D_CONV = D_MIX // 4
D_SC = D_MIX - D_ATTN - D_CONV
CONV_KERNEL = 31
SC_KERNEL = 3
D_FF = 2816
FFN_KERNEL = 3
RMS_EPS = 1e-6
LN_EPS = 1e-5
IN_SPLITS = (D_ATTN, D_ATTN, D_ATTN, ATTN_HEADS,
             D_CONV, D_CONV,
             D_SC, D_SC, D_SC)
D_IN = sum(IN_SPLITS)
NEG_INF = -1e30


def rms_norm(x, g):
    xf = x.astype(jnp.float32)
    y = xf * lax.rsqrt(jnp.mean(xf * xf, axis=-1, keepdims=True) + RMS_EPS)
    return (y * g.astype(jnp.float32)).astype(x.dtype)

def head_rms_norm(y, g):
    b, l, d = y.shape
    yf = y.astype(jnp.float32).reshape(b, l, d // GROUP_HEAD_DIM, GROUP_HEAD_DIM)
    yf = yf * lax.rsqrt(jnp.mean(yf * yf, axis=-1, keepdims=True) + RMS_EPS)
    return (yf.reshape(b, l, d) * g.astype(jnp.float32)).astype(y.dtype)

def layer_norm(x, g, b):
    xf = x.astype(jnp.float32)
    mu = jnp.mean(xf, axis=-1, keepdims=True)
    var = jnp.mean(jnp.square(xf - mu), axis=-1, keepdims=True)
    y = (xf - mu) * lax.rsqrt(var + LN_EPS)
    return (y * g.astype(jnp.float32) + b.astype(jnp.float32)).astype(x.dtype)

def causal_depthwise_conv(x, w):
    k, c = w.shape
    return lax.conv_general_dilated(
        x, w[:, None, :].astype(x.dtype), window_strides=(1,),
        padding=[(k - 1, 0)], dimension_numbers=("NWC", "WIO", "NWC"),
        feature_group_count=c)

def forgetting_attention(q, k, v, log_f):
    L = q.shape[1]
    scale = ATTN_HEAD_DIM ** -0.5
    F = jnp.cumsum(log_f, axis=1).transpose(0, 2, 1)

    def attend(start, end):
        qb = q[:, start:end]
        s = jnp.einsum("bqhd,bkhd->bhqk", qb, k[:, :end],
                       preferred_element_type=jnp.float32) * scale
        s = s + F[:, :, start:end, None] - F[:, :, None, :end]
        mask = jnp.arange(start, end)[:, None] >= jnp.arange(end)[None, :]
        s = jnp.where(mask, s, NEG_INF)
        p = jax.nn.softmax(s, axis=-1)
        return jnp.einsum("bhqk,bkhd->bqhd", p.astype(v.dtype), v[:, :end])

    outs = [attend(0, N_META)]
    for i in range((L - N_META) // Q_BLOCK):
        start = N_META + i * Q_BLOCK
        outs.append(attend(start, start + Q_BLOCK))
    return jnp.concatenate(outs, axis=1)

def mixer_sublayer(h, pre_g, post_g, w_in, b_forget, a_dw_w, a_dw_b, a_ln_g,
                   a_ln_b, a_pw_w, sc_conv_w, head_g, w_out):
    bsz, L, _ = h.shape
    u = rms_norm(h, pre_g)
    z = jnp.einsum("bld,de->ble", u, w_in)
    idx = np.cumsum(IN_SPLITS)[:-1].tolist()
    q, k, v, f_logit, a_val, a_gate, sc_b, sc_c, sc_x = jnp.split(z, idx, axis=-1)

    log_f = jax.nn.log_sigmoid((f_logit + b_forget).astype(jnp.float32))
    hs = (bsz, L, ATTN_HEADS, ATTN_HEAD_DIM)
    y_attn = forgetting_attention(q.reshape(hs), k.reshape(hs), v.reshape(hs), log_f)
    y_attn = y_attn.reshape(bsz, L, D_ATTN)

    a = a_val * jax.nn.sigmoid(a_gate)
    a = causal_depthwise_conv(a, a_dw_w) + a_dw_b
    a = jax.nn.silu(layer_norm(a, a_ln_g, a_ln_b))
    y_conv = jnp.einsum("blc,ce->ble", a, a_pw_w)

    y_sc = sc_b * causal_depthwise_conv(sc_c * sc_x, sc_conv_w)

    y = jnp.concatenate([y_attn, y_conv, y_sc], axis=-1)
    y = jnp.einsum("ble,ed->bld", head_rms_norm(y, head_g), w_out)
    return h + rms_norm(y, post_g)

def ffn_sublayer(h, pre_g, post_g, w_up, conv_w, w_down):
    u = rms_norm(h, pre_g)
    z = jnp.einsum("bld,df->blf", u, w_up)
    z = causal_depthwise_conv(z, conv_w)
    g, up = jnp.split(z, 2, axis=-1)
    y = jnp.einsum("blf,fd->bld", jax.nn.silu(g) * up, w_down)
    return h + rms_norm(y, post_g)

def first_inputs(seed: int = 0) -> dict:
    key = jax.random.key(seed)
    ks = jax.random.split(key, 20)
    f32 = jnp.float32

    def nrm(k, shape, scale):
        return jax.random.normal(k, shape, f32) * scale

    def gain(k, shape):
        return 1.0 + 0.05 * jax.random.normal(k, shape, f32)

    x = jax.random.normal(ks[0], (BATCH, SEQ, D_MODEL), f32)
    meta_tokens = nrm(ks[1], (N_META, D_MODEL), 1.0)
    col_scale = np.ones((D_IN,), np.float32)
    f0 = 3 * D_ATTN
    col_scale[f0:f0 + ATTN_HEADS] = 0.1
    w_in = nrm(ks[2], (DEPTH, D_MODEL, D_IN), D_MODEL ** -0.5) * jnp.asarray(col_scale)
    b_forget = jax.random.uniform(ks[3], (DEPTH, ATTN_HEADS), f32, 3.0, 6.0)
    return {
        "x": x,
        "meta_tokens": meta_tokens,
        "mix_pre_g": gain(ks[4], (DEPTH, D_MODEL)),
        "mix_post_g": gain(ks[5], (DEPTH, D_MODEL)),
        "w_in": w_in,
        "b_forget": b_forget,
        "a_dw_w": nrm(ks[6], (DEPTH, CONV_KERNEL, D_CONV), CONV_KERNEL ** -0.5),
        "a_dw_b": nrm(ks[7], (DEPTH, D_CONV), 0.02),
        "a_ln_g": gain(ks[8], (DEPTH, D_CONV)),
        "a_ln_b": nrm(ks[9], (DEPTH, D_CONV), 0.02),
        "a_pw_w": nrm(ks[10], (DEPTH, D_CONV, D_CONV), D_CONV ** -0.5),
        "sc_conv_w": nrm(ks[11], (DEPTH, SC_KERNEL, D_SC), SC_KERNEL ** -0.5),
        "head_g": gain(ks[12], (DEPTH, D_MIX)),
        "w_out": nrm(ks[13], (DEPTH, D_MIX, D_MODEL), D_MIX ** -0.5),
        "ffn_pre_g": gain(ks[14], (DEPTH, D_MODEL)),
        "ffn_post_g": gain(ks[15], (DEPTH, D_MODEL)),
        "ffn_w_up": nrm(ks[16], (DEPTH, D_MODEL, 2 * D_FF), D_MODEL ** -0.5),
        "ffn_conv_w": nrm(ks[17], (DEPTH, FFN_KERNEL, 2 * D_FF), FFN_KERNEL ** -0.5),
        "ffn_w_down": nrm(ks[18], (DEPTH, D_FF, D_MODEL), D_FF ** -0.5),
    }

def first_block(x, meta_tokens, mix_pre_g, mix_post_g, w_in, b_forget, a_dw_w,
              a_dw_b, a_ln_g, a_ln_b, a_pw_w, sc_conv_w, head_g, w_out,
              ffn_pre_g, ffn_post_g, ffn_w_up, ffn_conv_w, ffn_w_down):
    bsz = x.shape[0]
    meta = jnp.broadcast_to(meta_tokens[None].astype(x.dtype), (bsz, N_META, x.shape[-1]))
    h = jnp.concatenate([meta, x], axis=1)
    for l in range(DEPTH):
        h = mixer_sublayer(h, mix_pre_g[l], mix_post_g[l], w_in[l], b_forget[l],
                           a_dw_w[l], a_dw_b[l], a_ln_g[l], a_ln_b[l], a_pw_w[l],
                           sc_conv_w[l], head_g[l], w_out[l])
        h = ffn_sublayer(h, ffn_pre_g[l], ffn_post_g[l], ffn_w_up[l],
                         ffn_conv_w[l], ffn_w_down[l])
    return h[:, N_META:]


DEPTH_2 = 1

GRID_W = 64
CTX_LEN = 256

M_HEADS = 8
M_QK_DIM = 64
M_V_DIM = 128
M_QK = M_HEADS * M_QK_DIM
M_V = M_HEADS * M_V_DIM
M_CHUNK = 64

H_HEADS = 8
H_K_DIM = 128
H_V_DIM = 128
H_K = H_HEADS * H_K_DIM
H_V = H_HEADS * H_V_DIM
H_CHUNK = 16

FFN_HIDDEN = 2816
N_MOD = 9
EPS = 1e-6

PROJ_SIZES = (M_QK, M_QK, M_V, M_V, 2 * M_HEADS, 2 * M_HEADS,
              H_K, 2 * H_K, H_V, H_V, D_MODEL, D_MODEL)


def _rms(x, g):
    xf = x.astype(jnp.float32)
    y = xf * lax.rsqrt(jnp.mean(xf * xf, axis=-1, keepdims=True) + EPS)
    return y.astype(x.dtype) * g

def _head_rms(y, g, heads):
    B, T, W = y.shape
    return _rms(y.reshape(B, T, heads, W // heads), g.reshape(heads, W // heads)).reshape(B, T, W)

def _modulate(xn, shift, scale):
    return xn * (1.0 + scale) + shift

def _swiglu(xm, w_in, w_out):
    a, u = jnp.split(xm @ w_in, 2, axis=-1)
    return (jax.nn.silu(a) * u) @ w_out

def _split_proj(p):
    idx = np.cumsum(PROJ_SIZES)[:-1].tolist()
    return jnp.split(p, idx, axis=-1)

def _to_chunks(a, L):
    B, H, T = a.shape[:3]
    rest = a.shape[3:]
    return jnp.moveaxis(a.reshape(B, H, T // L, L, *rest), 2, 0)

def _from_chunks(a):
    NC, B, H, L = a.shape[:4]
    rest = a.shape[4:]
    return jnp.moveaxis(a, 0, 2).reshape(B, H, NC * L, *rest)

def _to_col_major(a):
    B, T, C = a.shape
    rows = T // GRID_W
    return a.reshape(B, rows, GRID_W, C).transpose(0, 2, 1, 3).reshape(B, T, C)

def _to_row_major(a):
    B, T, C = a.shape
    rows = T // GRID_W
    return a.reshape(B, GRID_W, rows, C).transpose(0, 2, 1, 3).reshape(B, T, C)

def _mlstm_scan(q, k, v, ig, fg, state):
    L = M_CHUNK
    mask = jnp.tril(jnp.ones((L, L), dtype=bool))
    scale = M_QK_DIM ** -0.5
    f32 = jnp.float32
    xs = (_to_chunks(q.astype(f32) * scale, L), _to_chunks(k.astype(f32), L),
          _to_chunks(v.astype(f32), L), _to_chunks(ig.astype(f32), L),
          _to_chunks(jax.nn.log_sigmoid(fg.astype(f32)), L))

    def body(carry, inp):
        C, n, m = carry
        qc, kc, vc, ic, lf = inp
        b = jnp.cumsum(lf, axis=-1)
        dlog = jnp.where(mask, b[..., :, None] - b[..., None, :] + ic[..., None, :], -jnp.inf)
        inter_log = b + m[..., None]
        m_t = jnp.maximum(inter_log, jnp.max(dlog, axis=-1))
        s = jnp.einsum('bhtd,bhsd->bhts', qc, kc) * jnp.exp(dlog - m_t[..., None])
        w_inter = jnp.exp(inter_log - m_t)
        num = w_inter[..., None] * jnp.einsum('bhtd,bhdv->bhtv', qc, C) + jnp.einsum('bhts,bhsv->bhtv', s, vc)
        den = w_inter * jnp.einsum('bhtd,bhd->bht', qc, n) + jnp.sum(s, axis=-1)
        h = num / jnp.maximum(jnp.abs(den), jnp.exp(-m_t))[..., None]
        b_last = b[..., -1]
        w_log = b_last[..., None] - b + ic
        m_new = jnp.maximum(b_last + m, jnp.max(w_log, axis=-1))
        decay = jnp.exp(b_last + m - m_new)
        w = jnp.exp(w_log - m_new[..., None])
        C_new = decay[..., None, None] * C + jnp.einsum('bhs,bhsd,bhsv->bhdv', w, kc, vc)
        n_new = decay[..., None] * n + jnp.einsum('bhs,bhsd->bhd', w, kc)
        return (C_new, n_new, m_new), h

    state, h = lax.scan(body, state, xs)
    return _from_chunks(h), state

def _hgrn_scan(q, k, v, logf, S):
    L = H_CHUNK
    mask = jnp.tril(jnp.ones((L, L), dtype=bool))[:, :, None]
    f32 = jnp.float32
    xs = tuple(_to_chunks(a.astype(f32), L) for a in (q, k, v, logf))

    def body(S, inp):
        qc, kc, vc, lf = inp
        b = jnp.cumsum(lf, axis=2)
        diff = b[:, :, :, None, :] - b[:, :, None, :, :]
        decay = jnp.exp(jnp.where(mask, diff, -jnp.inf))
        attn = jnp.einsum('bhtd,bhtsd,bhsd->bhts', qc, decay, kc)
        o = jnp.einsum('bhtd,bhdv->bhtv', qc * jnp.exp(b), S) + jnp.einsum('bhts,bhsv->bhtv', attn, vc)
        b_last = b[:, :, -1]
        S_new = jnp.exp(b_last)[..., None] * S + jnp.einsum(
            'bhsd,bhsv->bhdv', kc * jnp.exp(b_last[:, :, None, :] - b), vc)
        return S_new, o

    S, o = lax.scan(body, S, xs)
    return _from_chunks(o), S

def _flip_t(args):
    return tuple(jnp.flip(a, axis=2) for a in args)

def _bidir_scan(scan_fn, ctx_fwd, ctx_bwd, lat_fwd, lat_bwd, init):
    hcf, s_f = scan_fn(*ctx_fwd, init)
    hlf, _ = scan_fn(*lat_fwd, s_f)
    hcb, s_b = scan_fn(*_flip_t(ctx_bwd), init)
    hlb, _ = scan_fn(*_flip_t(lat_bwd), s_b)
    return hcf + jnp.flip(hcb, axis=2), hlf + jnp.flip(hlb, axis=2)

def _mlstm_branch(seg_c, seg_l, gain, dtype):
    f32 = jnp.float32

    def prep(seg):
        q, k, v, o, ig, fg = seg
        B, T, _ = q.shape
        hd = lambda a: a.reshape(B, T, M_HEADS, -1).transpose(0, 2, 1, 3)
        ig = ig.astype(f32).transpose(0, 2, 1)
        fg = fg.astype(f32).transpose(0, 2, 1)
        qh, kh, vh = hd(q), hd(k), hd(v)
        fwd = (qh, kh, vh, ig[:, :M_HEADS], fg[:, :M_HEADS])
        bwd = (qh, kh, vh, ig[:, M_HEADS:], fg[:, M_HEADS:])
        return fwd, bwd, o

    cf, cb, oc = prep(seg_c)
    lf, lb, ol = prep(seg_l)
    B = oc.shape[0]
    init = (jnp.zeros((B, M_HEADS, M_QK_DIM, M_V_DIM), f32),
            jnp.zeros((B, M_HEADS, M_QK_DIM), f32),
            jnp.zeros((B, M_HEADS), f32))
    hc, hl = _bidir_scan(_mlstm_scan, cf, cb, lf, lb, init)

    def out(h, o):
        B_, H, T, dv = h.shape
        h = h.transpose(0, 2, 1, 3).reshape(B_, T, H * dv)
        return (_head_rms(h, gain, M_HEADS) * jax.nn.sigmoid(o.astype(f32))).astype(dtype)

    return out(hc, oc), out(hl, ol)

def _hgrn_gates(f_pre, lb):
    fp = f_pre.astype(jnp.float32)
    logf = jnp.log(lb + (1.0 - lb) * jax.nn.sigmoid(fp))
    k = (1.0 - lb) * jax.nn.sigmoid(-fp)
    return logf, k

def _hgrn_branch(seg_c, seg_l, lb, gain, dtype):
    f32 = jnp.float32

    def prep(seg):
        q, f, i, g = seg
        B, T, _ = q.shape
        hd = lambda a: a.astype(f32).reshape(B, T, H_HEADS, -1).transpose(0, 2, 1, 3)
        qh = hd(jax.nn.silu(q.astype(f32)))
        vh = hd(i)
        lf_f, k_f = _hgrn_gates(f[..., :H_K], lb[0])
        lf_b, k_b = _hgrn_gates(f[..., H_K:], lb[1])
        return (qh, hd(k_f), vh, hd(lf_f)), (qh, hd(k_b), vh, hd(lf_b)), g

    cf, cb, gc = prep(seg_c)
    lf, lbw, gl = prep(tuple(_to_col_major(a) for a in seg_l))
    B = gc.shape[0]
    init = jnp.zeros((B, H_HEADS, H_K_DIM, H_V_DIM), f32)
    hc, hl = _bidir_scan(_hgrn_scan, cf, cb, lf, lbw, init)

    def out(h, g):
        B_, H, T, dv = h.shape
        h = h.transpose(0, 2, 1, 3).reshape(B_, T, H * dv)
        return (_head_rms(h, gain, H_HEADS) * jax.nn.silu(g.astype(f32))).astype(dtype)

    return out(hc, gc), _to_row_major(out(hl, gl))

def _token_mix(xc, xl, w_in, b_in, m_gain, lb, h_gain, proj_m, proj_h, w_out, need_ctx):
    seg_c = _split_proj(xc @ w_in + b_in)
    seg_l = _split_proj(xl @ w_in + b_in)
    hm_c, hm_l = _mlstm_branch(seg_c[0:6], seg_l[0:6], m_gain, xl.dtype)
    hh_c, hh_l = _hgrn_branch(seg_c[6:10], seg_l[6:10], lb, h_gain, xl.dtype)

    def merge(hm, hh, gm, gh):
        return (jax.nn.sigmoid(gm) * (hm @ proj_m) + jax.nn.sigmoid(gh) * (hh @ proj_h)) @ w_out

    y_l = merge(hm_l, hh_l, seg_l[10], seg_l[11])
    y_c = merge(hm_c, hh_c, seg_c[10], seg_c[11]) if need_ctx else None
    return y_c, y_l

def second_inputs(seed: int = 0) -> dict:
    key = jax.random.key(seed)
    ks = jax.random.split(key, 24)
    D, F = D_MODEL, FFN_HIDDEN
    P = int(sum(PROJ_SIZES))
    nrm = lambda k, shape, s: jax.random.normal(k, shape, jnp.float32) * s
    gains = lambda k, shape: 1.0 + nrm(k, shape, 0.05)
    f_start = int(sum(PROJ_SIZES[:5]))
    f_bias = jnp.tile(jnp.linspace(3.0, 6.0, M_HEADS), 2)
    b_off = jnp.zeros((P,), jnp.float32).at[f_start:f_start + 2 * M_HEADS].set(f_bias)
    return {
        "x": nrm(ks[0], (BATCH, SEQ, D), 1.0),
        "c": nrm(ks[1], (BATCH, D), 1.0),
        "ctx": nrm(ks[2], (BATCH, CTX_LEN, D), 1.0),
        "c_ctx": nrm(ks[3], (D,), 1.0),
        "ada_w": nrm(ks[4], (DEPTH_2, D, N_MOD * D), D ** -0.5),
        "ada_b": nrm(ks[5], (DEPTH_2, N_MOD * D), 0.02),
        "ffn1_norm": gains(ks[6], (DEPTH_2, D)),
        "ffn1_w_in": nrm(ks[7], (DEPTH_2, D, 2 * F), D ** -0.5),
        "ffn1_w_out": nrm(ks[8], (DEPTH_2, F, D), F ** -0.5),
        "mix_norm": gains(ks[9], (DEPTH_2, D)),
        "mix_w_in": nrm(ks[10], (DEPTH_2, D, P), D ** -0.5),
        "mix_b_in": b_off[None, :] + nrm(ks[11], (DEPTH_2, P), 0.02),
        "mlstm_norm": gains(ks[12], (DEPTH_2, M_V)),
        "hgrn_lb_logits": nrm(ks[13], (2, DEPTH_2 + 1, H_K), 0.5),
        "hgrn_norm": gains(ks[14], (DEPTH_2, H_V)),
        "proj_m": nrm(ks[15], (DEPTH_2, M_V, D), M_V ** -0.5),
        "proj_h": nrm(ks[16], (DEPTH_2, H_V, D), H_V ** -0.5),
        "mix_w_out": nrm(ks[17], (DEPTH_2, D, D), D ** -0.5),
        "ffn2_norm": gains(ks[18], (DEPTH_2, D)),
        "ffn2_w_in": nrm(ks[19], (DEPTH_2, D, 2 * F), D ** -0.5),
        "ffn2_w_out": nrm(ks[20], (DEPTH_2, F, D), F ** -0.5),
        "final_norm": gains(ks[21], (D,)),
    }

def second_block(x, c, ctx, c_ctx, ada_w, ada_b, ffn1_norm, ffn1_w_in, ffn1_w_out, mix_norm,
              mix_w_in, mix_b_in, mlstm_norm, hgrn_lb_logits, hgrn_norm, proj_m, proj_h,
              mix_w_out, ffn2_norm, ffn2_w_in, ffn2_w_out, final_norm):
    B = x.shape[0]
    D = x.shape[-1]
    lb_all = jnp.cumsum(jax.nn.softmax(hgrn_lb_logits.astype(jnp.float32), axis=1), axis=1)
    h = ctx
    for l in range(DEPTH_2):
        last = l == DEPTH_2 - 1
        ml = (jax.nn.silu(c) @ ada_w[l] + ada_b[l]).reshape(B, N_MOD, 1, D)
        mc = (jax.nn.silu(c_ctx) @ ada_w[l] + ada_b[l]).reshape(N_MOD, 1, 1, D)
        x = x + 0.5 * ml[:, 2] * _swiglu(_modulate(_rms(x, ffn1_norm[l]), ml[:, 0], ml[:, 1]), ffn1_w_in[l], ffn1_w_out[l])
        h = h + 0.5 * mc[2] * _swiglu(_modulate(_rms(h, ffn1_norm[l]), mc[0], mc[1]), ffn1_w_in[l], ffn1_w_out[l])
        y_c, y_l = _token_mix(_modulate(_rms(h, mix_norm[l]), mc[3], mc[4]),
                              _modulate(_rms(x, mix_norm[l]), ml[:, 3], ml[:, 4]),
                              mix_w_in[l], mix_b_in[l], mlstm_norm[l], lb_all[:, l], hgrn_norm[l],
                              proj_m[l], proj_h[l], mix_w_out[l], not last)
        x = x + ml[:, 5] * y_l
        if not last:
            h = h + mc[5] * y_c
            h = h + 0.5 * mc[8] * _swiglu(_modulate(_rms(h, ffn2_norm[l]), mc[6], mc[7]), ffn2_w_in[l], ffn2_w_out[l])
        x = x + 0.5 * ml[:, 8] * _swiglu(_modulate(_rms(x, ffn2_norm[l]), ml[:, 6], ml[:, 7]), ffn2_w_in[l], ffn2_w_out[l])
    return _rms(x, final_norm)


def setup_inputs(seed=0):
    out = dict(first_inputs(seed))
    for name, value in second_inputs(seed + 1).items():
        if name != "x":
            out[name + "_2"] = value
    return out


def reference(
    x, meta_tokens, mix_pre_g, mix_post_g, w_in, b_forget, a_dw_w, a_dw_b, a_ln_g, a_ln_b,
    a_pw_w, sc_conv_w, head_g, w_out, ffn_pre_g, ffn_post_g, ffn_w_up, ffn_conv_w, ffn_w_down,
    c_2, ctx_2, c_ctx_2, ada_w_2, ada_b_2, ffn1_norm_2, ffn1_w_in_2, ffn1_w_out_2, mix_norm_2,
    mix_w_in_2, mix_b_in_2, mlstm_norm_2, hgrn_lb_logits_2, hgrn_norm_2, proj_m_2, proj_h_2,
    mix_w_out_2, ffn2_norm_2, ffn2_w_in_2, ffn2_w_out_2, final_norm_2,
):
    x = first_block(
        x, meta_tokens, mix_pre_g, mix_post_g, w_in, b_forget, a_dw_w, a_dw_b, a_ln_g, a_ln_b,
        a_pw_w, sc_conv_w, head_g, w_out, ffn_pre_g, ffn_post_g, ffn_w_up, ffn_conv_w,
        ffn_w_down,
    )
    return second_block(
        x, c_2, ctx_2, c_ctx_2, ada_w_2, ada_b_2, ffn1_norm_2, ffn1_w_in_2, ffn1_w_out_2,
        mix_norm_2, mix_w_in_2, mix_b_in_2, mlstm_norm_2, hgrn_lb_logits_2, hgrn_norm_2,
        proj_m_2, proj_h_2, mix_w_out_2, ffn2_norm_2, ffn2_w_in_2, ffn2_w_out_2, final_norm_2,
    )


_drawn_inputs = setup_inputs


def setup_inputs(seed=0):
    import zlib

    import numpy as np

    out = dict(_drawn_inputs(seed))
    spreads = {}
    factors = {'a_ln_b': 4.203,
     'ada_b_2': 4.217,
     'ffn1_norm_2': 5.877,
     'mix_norm_2': 4.338,
     'mlstm_norm_2': 61.347,
     'hgrn_lb_logits_2': 8.0,
     'hgrn_norm_2': 8.0,
     'ffn2_norm_2': 5.898}
    for name, (base, spread) in spreads.items():
        noise = np.random.default_rng([zlib.crc32(name.encode()), seed]).standard_normal(out[name].shape)
        drawn = base * np.exp(spread * noise) if base else spread * noise
        out[name] = jnp.asarray(drawn.astype(out[name].dtype))
    for name, factor in factors.items():
        out[name] = (out[name] * factor).astype(out[name].dtype)
    return out
```

```python
import contextlib
from contextlib import ExitStack

import numpy as np
import concourse.bass as bass
from concourse import mybir

F32 = mybir.dt.float32
U8 = mybir.dt.uint8
ALU = mybir.AluOpType
ACT = mybir.ActivationFunctionType
AX_X = mybir.AxisListType.X

P = 128
D = 1024
KD = D // P
META = 16
SEQ = 256
T1 = META + SEQ
LAYERS = 2
HEADS = 8
DH = 64
DCONV = 256
TAPS = 31
FF = 2816
KF = FF // P
SLOTS = 4
SK = KF // 2
SW = 256
RMS_EPS = 1e-6
LN_EPS = 1e-5
NEG = -1e30
TT = [(0, 128, 128), (128, 128, 256), (256, 16, 272)]
C_PRE, C_POST, C_HEAD, C_FPRE, C_FPOST, C_DWB, C_LNG, C_LNB, C_DW = 0, 8, 16, 24, 32, 40, 42, 44, 46
C_SC = C_DW + 2 * TAPS
G0 = C_SC + 2 * 3
C_FC = G0
C_BF = C_FC + 3 * 2 * KF
NPAR = C_BF + 1
(B_ADA, B_N1, B_N2, B_ML, B_HG, B_N3, B_FIN) = (0, 72, 80, 88, 96, 104, 112)
B_MQ, B_MK, B_LB, B_HQ, B_HF, B_HGATE, B_GM, B_GH = 120, 124, 128, 160, 168, 184, 192, 200
B_IF = 208
NPAR2 = 210
NMOD = 9
PAIRS = HEADS // 2
VW = 129


class Count:

    def __init__(self, eng, name, S, rises):
        self.eng, self.name, self.S, self.rises = eng, name, S, rises
        self.count = {}
        self.turns = []
        self.loops = 0

    def now(self, sem):
        v = self.count.get(sem.name, 0)
        for var, key in self.turns:
            rise = self.rises.get(key, {}).get(sem.name, 0)
            if rise:
                v = v + var * rise
        return v

    def skip(self, sem, n=1):
        self.count[sem.name] = self.count.get(sem.name, 0) + n

    def next(self, sem, n=1):
        self.skip(sem, n)
        return self.now(sem)

    def inc(self, sem, n=1):
        self.skip(sem, n)
        return n

    def fence(self):
        if self.turns:
            self.eng.sem_inc(self.S.passed[self.name], 1)

    @contextlib.contextmanager
    def loop(self, n):
        key = (self.name, self.loops)
        self.loops += 1
        before = dict(self.count)
        self.fence()
        with self.eng.Fori(0, n) as i:
            self.turns.append((i, key))
            yield i
            self.fence()
            self.turns.pop()
        rise = {x: c - before.get(x, 0) for x, c in self.count.items()}
        self.rises[key] = rise
        for x, d in rise.items():
            self.count[x] += d * (n - 1)

    def leave(self, place):
        self.rises[place] = {x: c for x, c in self.count.items() if x.startswith(("half", "done"))}
        self.rises[place].update({x: c + 1 for x, c in self.count.items() if x.startswith("free")})

    def meet(self, place):
        self.count.update(self.rises[place])


class Semaphores:

    def __init__(self, new):
        self.order_act = new("order_act")
        self.order_dve = new("order_dve")
        self.order_pool = new("order_pool")
        self.consts = new("consts")
        self.x_in = new("x_in")
        self.tr_full = new("tr_full")
        self.tr_done = new("tr_done")
        self.par_ready = new("par_ready")
        self.sq = new("sq")
        self.stat = new("stat")
        self.rs = new("rs")
        self.u = new("u")
        self.gate = new("gate")
        self.conv = new("conv")
        self.mean = new("mean")
        self.xc = new("xc")
        self.xcsq = new("xcsq")
        self.var = new("var")
        self.cvrs = new("cvrs")
        self.xn = new("xn")
        self.cact = new("cact")
        self.f_act = new("f_act")
        self.f_ready = new("f_ready")
        self.vt = new("vt")
        self.sc_in = new("sc_in")
        self.ysc = new("ysc")
        self.s_full = new("s_full")
        self.s_ready = new("s_ready")
        self.p_exp = new("p_exp")
        self.p_norm = new("p_norm")
        self.pt_full = new("pt_full")
        self.pt_ready = new("pt_ready")
        self.yt_full = new("yt_full")
        self.hsq = new("hsq")
        self.hstat = new("hstat")
        self.hrs = new("hrs")
        self.yh = new("yh")
        self.ysq = new("ysq")
        self.h_new = new("h_new")
        self.z = new("z")
        self.z_used = new("z_used")
        self.cg = new("cg")
        self.sg = new("sg")
        self.hid = new("hid")
        self.sg2 = new("sg2")
        self.out_ready = new("out_ready")
        self.out_done = new("out_done")
        self.par2_ready = new("par2_ready")
        self.cc = new("cc")
        self.mod_ready = new("mod_ready")
        self.ada_rows = new("ada_rows")
        self.ada_full = new("ada_full")
        self.x2_ready = new("x2_ready")
        self.un = new("un")
        self.up = new("up")
        self.gate_in = new("gate_in")
        self.gate_m = new("gate_m")
        self.gate_exp = new("gate_exp")
        self.tg_full = new("tg_full")
        self.tg_ready = new("tg_ready")
        self.mrow = new("mrow")
        self.wb_full = new("wb_full")
        self.kw = new("kw")
        self.mv = new("mv")
        self.st_full = new("st_full")
        self.nm_full = new("nm_full")
        self.e_exp = new("e_exp")
        self.e_ready = new("e_ready")
        self.num_full = new("num_full")
        self.hs = new("hs")
        self.mrs = new("mrs")
        self.hm = new("hm")
        self.mt_full = new("mt_full")
        self.hq = new("hq")
        self.sig = new("sig")
        self.kk = new("kk")
        self.kc = new("kc")
        self.kct_full = new("kct_full")
        self.kct = new("kct")
        self.lev_ready = new("lev_ready")
        self.lev_full = new("lev_full")
        self.top = new("top")
        self.inter = new("inter")
        self.at = new("at")
        self.s0_full = new("s0_full")
        self.s0 = new("s0")
        self.o_full = new("o_full")
        self.osq = new("osq")
        self.omean = new("omean")
        self.ors = new("ors")
        self.hi = new("hi")
        self.hhd = new("hhd")
        self.mrg = new("mrg")
        self.land = [new(f"land{r}") for r in range(SLOTS)]
        self.half = [new(f"half{r}") for r in range(SLOTS)]
        self.done = [new(f"done{r}") for r in range(SLOTS)]
        self.free = [new(f"free{b}") for b in range(8)]
        self.passed = {n: new(f"passed_{n}") for n in ("pe", "act", "dve", "pool", "sp")}


def first_and_second_block(nc, rises, a, out):
    ctx = ExitStack()
    with ctx:
        def sb(name, shape, dt=F32):
            return ctx.enter_context(nc.sbuf_tensor(name, shape, dt))

        S = Semaphores(lambda name: ctx.enter_context(nc.semaphore(name)))
        bank = [ctx.enter_context(nc.psum_tensor(f"bank{b}", [P, 512], F32)) for b in range(8)]

        W = [sb(f"W{r}", [P, SK, SW]) for r in range(SLOTS)]
        ident = sb("ident", [P, P])
        mean_d = sb("mean_d", [P, P])
        mean_c = sb("mean_c", [P, P])
        mean_g = sb("mean_g", [P, P])
        neg_sel = sb("neg_sel", [HEADS, HEADS, P])
        eps_rms = sb("eps_rms", [P, 1])
        eps_ln = sb("eps_ln", [P, 1])
        ones_row = sb("ones_row", [P, T1])
        mask01 = sb("mask01", [P, 384])
        mask2 = sb("mask2", [16, T1])
        H1 = sb("H1", [P, KD, T1])
        H2 = sb("H2", [P, KD, 2 * SEQ])
        U = sb("U", [P, KD, 2 * SEQ])
        SQ = sb("SQ", [P, KD, 2 * SEQ])
        RS = sb("RS", [P, 2 * SEQ])
        LNT = sb("LNT", [P, 2 * SEQ])
        PL = sb("PL", [P, NPAR])
        tick = sb("tick", [P, 1])
        P2 = sb("P2", [P, NPAR2])
        MOD = sb("MOD", [P, NMOD, KD, 2])
        GS = sb("GS", [P, 3, KD, 2])
        GATE = sb("GATE", [P, 3, KD, 2])
        CC = sb("CC", [P, KD, 2])
        LBC = sb("LBC", [P, 4, 16])
        NB = sb("NB", [P, 16])
        MQB = sb("MQB", [P, 4])
        tri = sb("tri", [P, 2, P])
        neg_one = sb("neg_one", [40, 2, P])
        lmask = sb("lmask", [P, 7, 2, P], U8)
        ARENA_WORDS = 20400
        arena = sb("arena", [P, ARENA_WORDS])

        class Cut:
            def __init__(self):
                self.at = 0

            def __call__(self, *shape):
                n = int(np.prod(shape))
                v = arena[:, self.at:self.at + n]
                self.at += n
                assert self.at <= ARENA_WORDS, self.at
                if len(shape) == 2:
                    return v.rearrange("p (a b) -> p a b", a=shape[0])
                if len(shape) == 3:
                    return v.rearrange("p (a b c) -> p a b c", a=shape[0], b=shape[1])
                return v

        cut = Cut()
        XT = cut(5, D)
        CR = cut(P)
        cut = Cut()
        HID = cut(KF, T1)
        Y = cut(KD, T1)
        Z = cut(2, 4, T1)
        CZ = cut(4, T1)
        SG = cut(2, T1)
        TMP = cut(T1)
        cut.at = KF * T1 + KD * T1
        QT = cut(4, T1)
        KT = cut(4, T1)
        V = cut(3, 512)
        YC = cut(KD, T1)
        AV = cut(2, T1)
        AG = cut(2, T1)
        AP_ = cut(2, TAPS - 1 + T1)
        CV = cut(2, T1)
        CS = cut(2, T1)
        SCB = cut(2, T1)
        SCC = cut(2, T1)
        SCX = cut(2, T1)
        CX = cut(2, 2 + T1)
        FX = cut(T1)
        FT = cut(T1)
        FM = cut(T1)
        FC = cut(T1)
        cut.at = 0
        SC = [cut(384 + T1) for _ in range(2)]
        PR = [cut(384 + T1) for _ in range(2)]
        PT = [cut(432) for _ in range(2)]
        MX = [cut(4) for _ in range(2)]
        NM = [cut(4) for _ in range(2)]
        SM = [cut(4) for _ in range(2)]
        RC = [cut(4) for _ in range(2)]
        RSH = cut(KD, T1)
        assert cut.at <= KF * T1

        cut = Cut()
        HID2 = cut(KF, 2 * SEQ)
        SG2 = cut(2, 2, 2 * SEQ)
        UN = cut(KD, 2 * SEQ)
        cut = Cut()
        HG = cut(HEADS, SEQ)
        MRG = cut(HEADS, SEQ)
        GI, GF, GT_ = cut(2 * SEQ), cut(2 * SEQ), cut(2 * SEQ)
        GB = cut(2 * SEQ)
        G4 = cut(4, SEQ)
        GM = cut(SEQ)
        G1 = cut(8)
        TG = cut(8, 40)
        SEL2 = cut(8)
        MR = cut(2, 2, SEQ)
        m0 = cut.at
        MQ, MK, MKC = cut(SEQ), cut(SEQ), cut(2, P)
        MV = cut(4, 2, VW)
        MO = cut(2, SEQ)
        QW = cut(2, 2, SEQ)
        KW = cut(4, 2, DH)
        C0 = cut(2, VW)
        EE = cut(2, 6, P)
        DN, RD = cut(2, 4), cut(2, 4)
        HS, HM = cut(2, 2, P), cut(2, 2, P)
        SS, RR = cut(2, 2), cut(2, 2)
        cut.at = 2 * HEADS * SEQ
        HQ = cut(2, SEQ)
        HI = cut(4, 2 * P)
        FF_ = cut(2, 2, 2 * SEQ)
        KK = cut(2, 2, 2 * SEQ)
        SUF = cut(2, SEQ)
        SUFC = cut(2, SEQ)
        KC = cut(2, SEQ)
        QL = [cut(2, SEQ) for _ in range(2)]
        KL = [cut(2, SEQ) for _ in range(2)]
        AT = cut(2, 4, P)
        A128 = cut(2, 2, P)
        QR = cut(2, 2, SEQ)
        KCT = cut(2, 4, P)
        S0 = cut(2, 2, P)
        OSQ = cut(2 * SEQ)
        OT = cut(2 * SEQ)
        AR = [H2[0:2, 2 * q:2 * q + 2, 0:SEQ] for q in range(2)]
        AR += [U[0:2, 2 * q:2 * q + 2, 0:SEQ] for q in range(2)]
        modf = MOD[:, :, :, :].rearrange("p a b c -> p (a b) c")

        def ada_bank(j):
            return 2 + (j // 2 + 1) % 2

        UP = H1
        HMT = SQ[:, 0:4, :].rearrange("p a b -> p (a b)").rearrange("p (a b) -> p a b", a=KD)
        HHT = SQ[:, 4:8, :].rearrange("p a b -> p (a b)").rearrange("p (a b) -> p a b", a=KD)

        w_ada = a["ada_w_2"].rearrange("l (k p) n -> l p k n", p=P)[0]
        w_f1 = a["ffn1_w_in_2"].rearrange("l (k p) n -> l p k n", p=P)[0]
        w_f1o = a["ffn1_w_out_2"].rearrange("l (k p) n -> l p k n", p=P)[0]
        w_f2 = a["ffn2_w_in_2"].rearrange("l (k p) n -> l p k n", p=P)[0]
        w_f2o = a["ffn2_w_out_2"].rearrange("l (k p) n -> l p k n", p=P)[0]
        w_mix = a["mix_w_in_2"].rearrange("l (k p) n -> l p k n", p=P)[0]
        w_pm = a["proj_m_2"].rearrange("l (k p) n -> l p k n", p=P)[0]
        w_ph = a["proj_h_2"].rearrange("l (k p) n -> l p k n", p=P)[0]
        w_mo = a["mix_w_out_2"].rearrange("l (k p) n -> l p k n", p=P)[0]
        M_Q, M_K, M_V, M_O, M_IF, R_Q, R_F, R_I, R_G, G_M, G_H = (
            0, 512, 1024, 2048, 3072, 3104, 4128, 6176, 7200, 8224, 9248)

        w_in = a["w_in"].rearrange("l (k p) n -> l p k n", p=P)
        w_out = a["w_out"].rearrange("l (k p) n -> l p k n", p=P)
        w_up = a["ffn_w_up"].rearrange("l (k p) n -> l p k n", p=P)
        w_down = a["ffn_w_down"].rearrange("l (k p) n -> l p k n", p=P)
        pw = a["a_pw_w"].rearrange("l (k p) n -> l p k n", p=P)
        A0 = 3 * 512 + HEADS
        COL = dict(q=0, k=512, v=1024, f=1536, val=A0, gate=A0 + 256, sc_b=A0 + 512, sc_c=A0 + 768, sc_x=A0 + 1024)

        block = ctx.enter_context(nc.Block())

        @block.sync
        def _(eng):
            p = Count(eng, "sp", S, rises)
            x = a["x"][0]
            meta = a["meta_tokens"]
            ctxt = a["ctx_2"][0]
            for dst, src in ((XT[0:META, 0, :], meta), (XT[META:P, 0, :], x[0:P - META, :]),
                             (XT[:, 1, :], x[P - META:2 * P - META, :]), (XT[0:META, 2, :], x[2 * P - META:SEQ, :]),
                             (XT[:, 3, :], ctxt[0:P, :]), (XT[:, 4, :], ctxt[P:2 * P, :]),
                             (CR[0:KD, :], a["c_2"].rearrange("a (t p) -> (a t) p", p=P)),
                             (CR[KD:2 * KD, :], a["c_ctx_2"].rearrange("(t p) -> t p", p=P))):
                eng.dma_start(dst, src).then_inc(S.x_in, p.inc(S.x_in, 16))

            def load(r, src, dst=None):
                eng.wait_ge(S.done[r], p.next(S.done[r]))
                p.fence()
                k, n = src.shape[1], src.shape[2]
                eng.dma_start(W[r][:, 0:k, 0:n] if dst is None else dst, src).then_inc(S.land[r], p.inc(S.land[r], 16))

            with p.loop(LAYERS) as l:
                def vec(name, tiles):
                    return a[name].rearrange("l (t p) -> l t p", p=P)[l]

                eng.wait_ge(S.done[0], p.next(S.done[0]))
                p.fence()
                row = 0
                for name, n in (("mix_pre_g", 8), ("mix_post_g", 8), ("head_g", 8), ("ffn_pre_g", 8),
                                ("ffn_post_g", 8), ("a_dw_b", 2), ("a_ln_g", 2), ("a_ln_b", 2)):
                    src = a[name].rearrange("l (t p) -> l t p", p=P)[bass.ds(l, 1)].rearrange("a t p -> (a t) p")
                    eng.dma_start(W[0][row:row + n, 0, 0:P], src).then_inc(S.land[0], p.inc(S.land[0], 16))
                    row += n
                for name, n in (("a_dw_w", 2 * TAPS), ("sc_conv_w", 6)):
                    src = a[name].rearrange("l k (t p) -> l (k t) p", p=P)[bass.ds(l, 1)].rearrange("a t p -> (a t) p")
                    eng.dma_start(W[0][row:row + n, 0, 0:P], src).then_inc(S.land[0], p.inc(S.land[0], 16))
                    row += n
                fc = a["ffn_conv_w"].rearrange("l k (t p) -> l (k t) p", p=P)
                eng.dma_start(W[0][:, 0, P:2 * P], fc[bass.ds(l, 1), 0:P, :].rearrange("a t p -> (a t) p")).then_inc(S.land[0], p.inc(S.land[0], 16))
                eng.dma_start(W[0][0:4, 1, 0:P], fc[bass.ds(l, 1), P:P + 4, :].rearrange("a t p -> (a t) p")).then_inc(S.land[0], p.inc(S.land[0], 16))
                eng.dma_start(W[0][0:1, 1, P:P + HEADS], a["b_forget"][bass.ds(l, 1), :]).then_inc(S.land[0], p.inc(S.land[0], 16))

                def cols(t, c, n=SW, k0=0, k=KD):
                    return t[bass.ds(l, 1), :, k0:k0 + k, c:c + n].rearrange("a p k n -> (a p) k n")

                load(1, cols(w_in, COL["val"]))
                load(2, cols(w_in, COL["gate"]))
                load(3, cols(w_in, COL["f"], HEADS))
                load(0, cols(w_in, COL["q"]))
                load(1, cols(w_in, COL["q"] + SW))
                load(2, cols(w_in, COL["k"]))
                load(3, cols(w_in, COL["k"] + SW))
                load(0, cols(w_in, COL["v"]))
                load(1, cols(w_in, COL["v"] + SW))
                load(2, cols(w_in, COL["sc_c"]))
                load(3, cols(w_in, COL["sc_x"]))
                load(0, cols(w_in, COL["sc_b"]))
                load(1, cols(pw, 0, k=2))
                for n in range(2 * HEADS):
                    load((2 + n) % 4, w_ada[:, :, bass.ds(l * (4 * D) + n * SW, SW)])
                for c, r in enumerate((2, 3, 0, 1)):
                    load(r, cols(w_out, c * SW))

                def up(r, c):
                    for rr, base in ((r, 0), (r + 1, FF)):
                        load(rr, w_up[bass.ds(l, 1), :, :, bass.ds(base + c, SW)].rearrange("a p k n -> (a p) k n"))

                with p.loop(5) as i:
                    up(2, i * (2 * SW))
                    up(0, i * (2 * SW) + SW)
                up(2, 10 * SW)
                with p.loop(2) as i:
                    for j in range(2):
                        for half in range(2):
                            load(2 * j + half, w_down[bass.ds(l, 1), :, half * SK:(half + 1) * SK,
                                                      bass.ds(i * (2 * SW) + j * SW, SW)]
                                 .rearrange("a p k n -> (a p) k n"))
            eng.wait_ge(S.done[0], p.next(S.done[0]))
            row = 0
            rows = [("ada_b_2", 72), ("ffn1_norm_2", 8), ("mix_norm_2", 8), ("mlstm_norm_2", 8), ("hgrn_norm_2", 8),
                    ("ffn2_norm_2", 8)]
            for name, n in rows:
                eng.dma_start(W[0][row:row + n, 0, 0:P], a[name].rearrange("l (t p) -> (l t) p", p=P)).then_inc(S.land[0], p.inc(S.land[0], 16))
                row += n
            eng.dma_start(W[0][112:120, 0, 0:P], a["final_norm_2"].rearrange("(t p) -> t p", p=P)).then_inc(S.land[0], p.inc(S.land[0], 16))
            eng.dma_start(W[0][0:32, 0, P:2 * P], a["hgrn_lb_logits_2"].rearrange("d l (t p) -> (d l t) p", p=P)).then_inc(S.land[0], p.inc(S.land[0], 16))
            mb = a["mix_b_in_2"][0]
            for c, row in ((M_Q, B_MQ), (M_K, B_MK)):
                eng.dma_start(W[0][row:row + 4, 0, 0:P], mb[c:c + 4 * P].rearrange("(t p) -> t p", p=P)).then_inc(S.land[0], p.inc(S.land[0], 16))
            row = 32
            for c, n in ((R_Q, 8), (R_F, 16), (R_G, 8), (G_M, 8), (G_H, 8)):
                eng.dma_start(W[0][row:row + n, 0, P:2 * P], mb[c:c + n * P].rearrange("(t p) -> t p", p=P)).then_inc(S.land[0], p.inc(S.land[0], 16))
                row += n
            one = lambda c, n: mb[c:c + n].rearrange("(a n) -> a n", a=1)
            eng.dma_start(W[0][0:1, 1, 0:32], one(M_IF, 32)).then_inc(S.land[0], p.inc(S.land[0], 16))

            def bias(r, c, n=SW, at=0):
                src = a["mix_b_in_2"][0:1, bass.ds(c, n)]
                eng.dma_start(W[r][0:1, KD, at:at + n], src).then_inc(S.land[r], p.inc(S.land[r], 16))

            def strip(w, c, k0=0, k=KD, n=SW):
                return w[:, k0:k0 + k, bass.ds(c, n)] if not isinstance(c, int) else w[:, k0:k0 + k, c:c + n]

            for n, r in enumerate((1, 2, 3, 0)):
                load(r, strip(w_ada, 8 * D + n * SW))

            def ffn(w, wo, r0):
                def group(r, c):
                    load(r % 4, strip(w, c))
                    load((r + 1) % 4, strip(w, c + FF))
                with p.loop(5) as i:
                    group(r0, i * (2 * SW))
                    group(r0 + 2, i * (2 * SW) + SW)
                group(r0, 10 * SW)
                with p.loop(2) as i:
                    for j in range(2):
                        for half in range(2):
                            load((r0 + 2 + 2 * j + half) % 4, strip(wo, i * (2 * SW) + j * SW, half * SK, SK))

            ffn(w_f1, w_f1o, 1)
            load(3, strip(w_mix, M_IF, n=32))
            with p.loop(PAIRS) as i:
                eng.wait_ge(S.done[0], p.next(S.done[0]))
                p.fence()
                eng.dma_start(W[0][:, 0:KD, 0:P], strip(w_mix, i * P + M_Q, n=P)).then_inc(S.land[0], p.inc(S.land[0], 16))
                eng.dma_start(W[0][:, 0:KD, P:2 * P], strip(w_mix, i * P + M_K, n=P)).then_inc(S.land[0], p.inc(S.land[0], 16))
                bias(0, i * P + M_K, P, P)
                load(1, strip(w_mix, i * SW + M_V))
                bias(1, i * SW + M_V)
                load(2, strip(w_mix, i * SW + M_O))
                bias(2, i * SW + M_O)
                load(3, strip(w_mix, i * SW + R_G))
            with p.loop(PAIRS) as i:
                load(0, strip(w_mix, i * SW + R_Q))
                load(1, strip(w_mix, i * SW + R_F))
                load(2, strip(w_mix, i * SW + (R_F + D)))
                load(3, strip(w_mix, i * SW + R_I))
                bias(3, i * SW + R_I)
            with p.loop(PAIRS) as i:
                load(0, strip(w_mix, i * SW + G_M))
                load(1, strip(w_mix, i * SW + G_H))
                load(2, strip(w_pm, i * SW))
                load(3, strip(w_ph, i * SW))
            for r in range(4):
                load(r, strip(w_mo, r * SW))
            ffn(w_f2, w_f2o, 0)
            eng.wait_ge(S.out_ready, p.next(S.out_ready, 2))
            for t in range(2):
                eng.dma_start(out[0, t * P:(t + 1) * P, :], XT[:, t, :]).then_inc(S.out_done, p.inc(S.out_done, 16))
            eng.wait_ge(S.out_done, p.now(S.out_done))

        @block.gpsimd
        def _(eng):
            p = Count(eng, "pool", S, rises)

            def fill(v, x):
                eng.memset(v, x).then_inc(S.order_pool, p.inc(S.order_pool))
                eng.wait_ge(S.order_pool, p.now(S.order_pool))

            fill(ident[:, :], 0.0)
            eng.affine_select(out=ident[:, :], in_=ident[:, :], compare_op=ALU.not_equal, fill=1.0, base=0,
                                   pattern=[[-1, P]], channel_multiplier=1).then_inc(S.order_pool, p.inc(S.order_pool))
            eng.wait_ge(S.order_pool, p.now(S.order_pool))
            fill(eps_rms[:, :], RMS_EPS)
            fill(eps_ln[:, :], LN_EPS)
            eng.memset(LNT[:, :], 0.0).then_inc(S.consts, p.inc(S.consts))
            fill(mean_d[:, :], 1.0 / D)
            fill(mean_c[:, :], 1.0 / DCONV)
            fill(mean_g[:, :], 0.0)
            fill(mean_g[0:64, 0:64], 1.0 / 64)
            fill(mean_g[64:P, 64:P], 1.0 / 64)
            fill(neg_sel[:, :, :], 0.0)
            eng.affine_select(out=neg_sel[:, :, :], in_=neg_sel[:, :, :], compare_op=ALU.not_equal, fill=-1.0,
                                   base=0, pattern=[[-1, HEADS], [0, P]], channel_multiplier=1).then_inc(S.order_pool, p.inc(S.order_pool))
            eng.wait_ge(S.order_pool, p.now(S.order_pool))
            fill(ones_row[:, :], 1.0)
            fill(mask01[:, :], 0.0)
            for c in (0, 256):
                eng.affine_select(out=mask01[:, c:c + P], in_=mask01[:, c:c + P], compare_op=ALU.is_ge, fill=NEG,
                                       base=0, pattern=[[-1, P]], channel_multiplier=1).then_inc(S.order_pool, p.inc(S.order_pool))
                eng.wait_ge(S.order_pool, p.now(S.order_pool))
            fill(mask2[:, :], 0.0)
            eng.affine_select(out=mask2[:, :], in_=mask2[:, :], compare_op=ALU.is_ge, fill=NEG,
                                   base=256, pattern=[[-1, T1]], channel_multiplier=1).then_inc(S.consts, p.inc(S.consts))
            fill(neg_one[:, :, :], 0.0)
            for d in range(2):
                fill(neg_one[32 * d:32 * d + HEADS, d, :], -1.0)
            fill(tri[:, :, :], 1.0)
            eng.affine_select(out=tri[:, 0, :], in_=tri[:, 0, :], compare_op=ALU.is_ge, fill=0.0,
                                   base=0, pattern=[[1, P]], channel_multiplier=-1).then_inc(S.order_pool, p.inc(S.order_pool))
            eng.wait_ge(S.order_pool, p.now(S.order_pool))
            eng.affine_select(out=tri[:, 1, :], in_=tri[:, 1, :], compare_op=ALU.is_ge, fill=0.0,
                                   base=0, pattern=[[-1, P]], channel_multiplier=1).then_inc(S.order_pool, p.inc(S.order_pool))
            eng.wait_ge(S.order_pool, p.now(S.order_pool))
            for lev in range(7):
                h = 1 << lev
                nb = P // (2 * h)
                for d in range(2):
                    fill(H2[:, KD - 1, 0:P], 0.0)
                    q0 = h if d == 0 else 0
                    k0 = 0 if d == 0 else h
                    v = H2[:, KD - 1, 0:P].rearrange("p (n j) -> p n j", j=2 * h)[:, :, q0:q0 + h]
                    fill(v, 1.0)
                    eng.affine_select(out=v, in_=v, compare_op=ALU.is_ge, fill=0.0, base=-k0,
                                           pattern=[[-2 * h, nb], [0, h]], channel_multiplier=1).then_inc(S.order_pool, p.inc(S.order_pool))
                    eng.wait_ge(S.order_pool, p.now(S.order_pool))
                    eng.affine_select(out=v, in_=v, compare_op=ALU.is_ge, fill=0.0, base=k0 + h - 1,
                                           pattern=[[2 * h, nb], [0, h]], channel_multiplier=-1).then_inc(S.order_pool, p.inc(S.order_pool))
                    eng.wait_ge(S.order_pool, p.now(S.order_pool))
                    eng.tensor_copy(lmask[:, lev, d, :], H2[:, KD - 1, 0:P]).then_inc(S.order_pool, p.inc(S.order_pool))
                    eng.wait_ge(S.order_pool, p.now(S.order_pool))
            eng.sem_inc(S.consts, p.inc(S.consts))

        @block.tensor
        def _(eng):
            p = Count(eng, "pe", S, rises)
            for r in range(SLOTS):
                eng.sem_inc(S.done[r], 1)
                p.skip(S.done[r])
            for b in range(8):
                eng.sem_inc(S.free[b], 1)
            eng.wait_ge(S.consts, p.next(S.consts))
            mm = eng.matmul

            def take(b):
                eng.wait_ge(S.free[b], p.next(S.free[b]))

            eng.wait_ge(S.x_in, p.next(S.x_in, 128))
            widths = (P, P, META, P, P)
            for n, (t, half) in enumerate((t, half) for t in range(5) for half in range(2)):
                b, w = 4 + n % 4, widths[t]
                take(b)
                for k in range(4):
                    kk = 4 * half + k
                    last = eng.transpose(bank[b][:, k * w:(k + 1) * w], XT[0:w, t, kk * P:(kk + 1) * P], ident[0:w, 0:w])
                last.then_inc(S.tr_full, p.inc(S.tr_full))
            take(6)
            eng.transpose(bank[6][:, 0:2 * KD], CR[0:2 * KD, :], ident[0:2 * KD, 0:2 * KD]).then_inc(S.tr_full, p.inc(S.tr_full))
            eng.wait_ge(S.consts, p.next(S.consts))

            def stat(src, n, first, count, b=4, ready=S.sq, full=S.stat, lhs=None):
                take(b)
                for k in range(count):
                    eng.wait_ge(ready, p.next(ready))
                    last = mm(bank[b][:, 0:n], (mean_d if lhs is None else lhs)[:, :], src[:, k, 0:n],
                              start=k == 0, stop=k == count - 1)
                last.then_inc(full, p.inc(full))

            def slot_fm(r, rhs, n, k=KD, tiles=2, m=P, wait_u=False):
                eng.wait_ge(S.land[r], p.next(S.land[r], 16))
                for t in range(tiles):
                    b = 2 * (r % 2) + t
                    take(b)
                    for kk in range(k):
                        if wait_u and t == 0:
                            eng.wait_ge(S.u, p.next(S.u))
                        last = mm(bank[b][0:m, 0:n], W[r][:, kk, t * P:t * P + m], rhs(kk), start=kk == 0, stop=kk == k - 1)
                    sem = S.done[r] if t == tiles - 1 else S.half[r]
                    last.then_inc(sem, p.inc(sem))

            def u1(kk):
                return U[:, kk, 0:T1]

            def ada_products(b, half, r):
                eng.wait_ge(S.land[r], p.next(S.land[r], 16))
                for k in range(KD):
                    last = mm(bank[b][0:2, half * SW:(half + 1) * SW], CC[:, k, :], W[r][:, k, 0:SW],
                              start=k == 0, stop=k == KD - 1, skip_group_check=True)
                last.then_inc(S.done[r], p.inc(S.done[r]))

            def ada_columns(b, parity):
                eng.wait_ge(S.ada_rows, p.next(S.ada_rows))
                take(b)
                p.fence()
                for n in range(4):
                    last = eng.transpose(bank[b][:, 2 * n:2 * n + 2], AR[parity][:, n // 2, (n % 2) * P:(n % 2 + 1) * P], ident[0:2, 0:2])
                last.then_inc(S.ada_full, p.inc(S.ada_full))

            p.inc(S.cc)
            with p.loop(LAYERS) as l:
                take(4)
                eng.wait_ge(S.land[0], p.next(S.land[0], 16 * 13))
                eng.transpose(bank[4][:, 0:G0], W[0][0:G0, 0, 0:P], ident[0:G0, 0:G0])
                eng.transpose(bank[4][:, G0:G0 + P], W[0][:, 0, P:2 * P], ident[:, :])
                eng.transpose(bank[4][:, G0 + P:G0 + P + 4], W[0][0:4, 1, 0:P], ident[0:4, 0:4])
                eng.transpose(bank[4][0:HEADS, C_BF:C_BF + 1], W[0][0:1, 1, P:P + HEADS], ident[0:1, 0:1]).then_inc(S.done[0], p.inc(S.done[0]))
                stat(SQ, T1, True, KD)
                slot_fm(1, u1, T1, wait_u=True)
                slot_fm(2, u1, T1)
                slot_fm(3, u1, T1, tiles=1, m=HEADS)
                for r in (0, 1, 2, 3):
                    slot_fm(r, u1, T1)
                for r in (0, 1):
                    eng.wait_ge(S.land[r], p.next(S.land[r], 16))
                    b0 = 2 * (r % 2)
                    take(b0)
                    take(b0 + 1)
                    for i, (t0, w, _) in enumerate(TT):
                        o = bank[b0 + (i == 1)][0:w, (256 if i == 2 else 0):(512 if i == 2 else 256)]
                        for kk in range(KD):
                            last = mm(o, U[:, kk, t0:t0 + w], W[r][:, kk, 0:SW], start=kk == 0, stop=kk == KD - 1)
                    last.then_inc(S.done[r], p.inc(S.done[r]))
                slot_fm(2, u1, T1)
                stat(CV, T1, True, 2, b=6, ready=S.conv, full=S.mean, lhs=mean_c)
                slot_fm(3, u1, T1)
                stat(SQ, T1, True, 2, b=7, ready=S.xcsq, full=S.var, lhs=mean_c)
                slot_fm(0, u1, T1)
                eng.wait_ge(S.cact, p.next(S.cact, 2))
                slot_fm(1, lambda kk: CS[:, kk, :], T1, k=2)

                eng.wait_ge(S.f_ready, p.next(S.f_ready))
                eng.wait_ge(S.vt, p.next(S.vt, 4))

                def scores(j):
                    ba, bb = 4 + j % 2, 6 + j % 2
                    take(ba)
                    take(bb)
                    r0 = DH * (j % 2)
                    for i, (t0, w, end) in enumerate(TT):
                        o = (bank[ba][:, 0:128], bank[ba][:, 128:384], bank[bb][0:16, 0:T1])[i]
                        mm(o, QT[r0:r0 + DH, j // 2, t0:t0 + w], KT[r0:r0 + DH, j // 2, 0:end], start=True, stop=False)
                        last = mm(o, neg_sel[:, j, 0:w], FC[0:HEADS, 0:end], start=False, stop=True)
                    last.then_inc(S.s_full, p.inc(S.s_full))

                def weigh(j):
                    b, pr, pt = j % 2, PR[j % 2], PT[j % 2]
                    eng.wait_ge(S.p_norm, p.next(S.p_norm))
                    take(b)
                    for o, (t0, w), (c, n) in (((0, 128), (0, 128), (0, 128)), ((128, 256), (0, 128), (128, 128)),
                                               ((272, 400), (0, 128), (256, 128)), ((256, 272), (0, 16), (384, 128)),
                                               ((400, 416), (0, 16), (512, 128)), ((416, 432), (0, 16), (640, 16))):
                        last = eng.transpose(bank[b][0:n, o[0]:o[1]], pr[0:w, c:c + n], ident[0:w, 0:w])
                    last.then_inc(S.pt_full, p.inc(S.pt_full))
                    ada_products(ada_bank(j), 1, (3 + 2 * j) % 4)
                    yb = 2 + (j // 2) % 2
                    if j % 2 == 0:
                        take(yb)
                    eng.wait_ge(S.pt_ready, p.next(S.pt_ready))
                    r0 = DH * (j % 2)
                    cc = slice(j * DH, (j + 1) * DH)
                    mm(bank[yb][r0:r0 + DH, 0:272], V[:, 0, cc], pt[:, 0:272], start=True, stop=False)
                    mm(bank[yb][r0:r0 + DH, 128:272], V[:, 1, cc], pt[:, 272:416], start=False, stop=False)
                    last = mm(bank[yb][r0:r0 + DH, 256:272], V[0:16, 2, cc], pt[0:16, 416:432], start=False, stop=True)
                    if j % 2:
                        last.then_inc(S.yt_full, p.inc(S.yt_full))

                scores(0)
                for j in range(HEADS):
                    if j + 1 < HEADS:
                        scores(j + 1)
                    if j == 0:
                        eng.wait_ge(S.cc, p.now(S.cc))
                    else:
                        ada_columns(ada_bank(j - 1), (j - 1) % 2)
                    take(ada_bank(j))
                    ada_products(ada_bank(j), 0, (2 + 2 * j) % 4)
                    weigh(j)
                ada_columns(ada_bank(HEADS - 1), (HEADS - 1) % 2)
                for k in range(KD):
                    take(4 + k % 4)
                    eng.wait_ge(S.hsq, p.next(S.hsq))
                    mm(bank[4 + k % 4][:, 0:T1], mean_g[:, :], SQ[:, k, 0:T1], start=True, stop=True).then_inc(S.hstat, p.inc(S.hstat))
                for n, r in enumerate((2, 3, 0, 1)):
                    if n == 0:
                        eng.wait_ge(S.yh, p.next(S.yh, KD))
                    slot_fm(r, lambda kk: RSH[:, kk, :], T1)
                stat(SQ, T1, True, KD, ready=S.ysq)
                stat(SQ, T1, True, KD)
                eng.wait_ge(S.u, p.next(S.u, KD))
                with p.loop(5) as i:
                    for r in (2, 3, 0, 1):
                        slot_fm(r, u1, T1)
                slot_fm(2, u1, T1)
                slot_fm(3, u1, T1)
                eng.wait_ge(S.hid, p.next(S.hid, 11))

                def down(j, n):
                    for half in range(2):
                        r = 2 * j + half
                        eng.wait_ge(S.land[r], p.next(S.land[r], 16))
                        for t in range(2):
                            b = 2 * j + t
                            if half == 0:
                                take(b)
                            for kk in range(SK):
                                last = mm(bank[b][:, 0:n], W[r][:, kk, t * P:(t + 1) * P], HID[:, half * SK + kk, 0:n],
                                          start=half == 0 and kk == 0, stop=half == 1 and kk == SK - 1,
                                          skip_group_check=True)
                            if half == 1 and t == 0:
                                last.then_inc(S.half[r], p.inc(S.half[r]))
                        last.then_inc(S.done[r], p.inc(S.done[r]))

                with p.loop(2) as i:
                    down(0, T1)
                    down(1, T1)
                stat(SQ, T1, True, KD, ready=S.ysq)
                p.skip(S.h_new, 2 * KD)
            p.leave("second")
            eng.wait_ge(S.consts, p.next(S.consts))
            take(4)
            eng.wait_ge(S.land[0], p.next(S.land[0], 16 * 16))
            eng.transpose(bank[4][:, 0:P], W[0][:, 0, 0:P], ident[:, :])
            eng.transpose(bank[4][:, P:B_IF], W[0][0:B_IF - P, 0, P:2 * P], ident[0:B_IF - P, 0:B_IF - P])
            for g in range(2):
                for d in range(2):
                    last = mm(bank[4][32 * d:32 * d + 8, B_IF + g:B_IF + g + 1],
                              W[0][0:1, 1, 16 * g + 8 * d:16 * g + 8 * d + 8], ones_row[0:1, 0:1], start=True, stop=True,
                              skip_group_check=True)
            last.then_inc(S.done[0], p.inc(S.done[0]))
            for n, b in enumerate((0, 1)):
                take(b)
                ada_products(b, 0, 1 + 2 * n)
                ada_products(b, 1, (2 + 2 * n) % 4)
            for n, b in enumerate((0, 1)):
                ada_columns(b, 2 + n)
            p.leave("modulated")

            def u2(kk):
                return U[:, kk, :]

            def ffn(rhs, n, r0):
                stat(SQ, n, True, KD)
                eng.wait_ge(S.u, p.next(S.u, KD))
                with p.loop(5) as i:
                    for r in range(4):
                        slot_fm((r0 + r) % 4, rhs, n)
                slot_fm(r0, rhs, n)
                slot_fm(r0 + 1, rhs, n)
                eng.wait_ge(S.hid, p.next(S.hid, 11))
                with p.loop(2) as i:
                    for j in range(2):
                        for half in range(2):
                            r = (r0 + 2 + 2 * j + half) % 4
                            eng.wait_ge(S.land[r], p.next(S.land[r], 16))
                            for t in range(2):
                                b = 2 * j + t
                                if half == 0:
                                    take(b)
                                for kk in range(SK):
                                    last = mm(bank[b][:, 0:n], W[r][:, kk, t * P:(t + 1) * P],
                                              HID2[:, half * SK + kk, 0:n],
                                              start=half == 0 and kk == 0, stop=half == 1 and kk == SK - 1,
                                              skip_group_check=True)
                                if half == 1 and t == 0:
                                    last.then_inc(S.half[r], p.inc(S.half[r]))
                            last.then_inc(S.done[r], p.inc(S.done[r]))

            ffn(u2, 2 * SEQ, 1)
            stat(SQ, 2 * SEQ, True, KD)
            eng.wait_ge(S.u, p.next(S.u, KD))
            eng.wait_ge(S.up, p.next(S.up, KD))

            def group(o, pairs, bias=None):
                n = len(pairs)
                for i, (x, y) in enumerate(pairs):
                    last = mm(o, x, y, start=i == 0, stop=i == n - 1 and bias is None, skip_group_check=True)
                if bias is not None:
                    last = mm(o, bias[0], bias[1], start=False, stop=True, skip_group_check=True)
                return last

            p.leave("gates")
            eng.wait_ge(S.land[3], p.next(S.land[3], 16))
            take(0)
            take(1)
            for g in range(2):
                for d in range(2):
                    last = group(bank[g][32 * d:32 * d + 8, :],
                                 [(W[3][:, k, 16 * g + 8 * d:16 * g + 8 * d + 8], U[:, k, :]) for k in range(KD)])
            last.then_inc(S.done[3], p.inc(S.done[3]))
            eng.wait_ge(S.gate_exp, p.next(S.gate_exp))
            take(4)
            for i in range(8):
                last = eng.transpose(bank[4][:, 40 * i:40 * i + 40], G4[0:40, i // 2, (i % 2) * P:(i % 2 + 1) * P],
                                     ident[0:40, 0:40])
            last.then_inc(S.tg_full, p.inc(S.tg_full))
            eng.wait_ge(S.tg_ready, p.next(S.tg_ready))

            def token_tiles(r, tiles, banks):
                eng.wait_ge(S.land[r], p.next(S.land[r], 32))
                for b in banks:
                    take(b)
                for b, c, tok in tiles:
                    last = group(bank[b][:, c:c + SW], [(tok(k), W[r][:, k, :]) for k in range(KD)],
                                 (ones_row[0:1, 0:P], W[r][0:1, KD, :]))
                last.then_inc(S.done[r], p.inc(S.done[r]))

            def toks(t0):
                return lambda k: U[:, k, t0:t0 + P]

            def perm(t0):
                return lambda k: UP[:, k, t0:t0 + P]

            p.leave("memory")
            with p.loop(PAIRS) as i:
                eng.wait_ge(S.land[0], p.next(S.land[0], 48))
                take(0)
                take(1)
                group(bank[0][:, 0:SEQ], [(W[0][:, k, 0:P], U[:, k, 0:SEQ]) for k in range(KD)])
                group(bank[0][:, SEQ:2 * SEQ], [(W[0][:, k, P:2 * P], U[:, k, 0:SEQ]) for k in range(KD)])
                for t in range(2):
                    last = group(bank[1][:, t * P:(t + 1) * P],
                                 [(U[:, k, SEQ + t * P:SEQ + (t + 1) * P], W[0][:, k, P:2 * P]) for k in range(KD)],
                                 (ones_row[0:1, 0:P], W[0][0:1, KD, P:2 * P]))
                last.then_inc(S.done[0], p.inc(S.done[0]))
                token_tiles(1, [(2, 0, toks(0)), (2, SW, toks(P)), (3, 0, toks(2 * P)), (3, SW, toks(3 * P))], (2, 3))
                eng.wait_ge(S.mrow, p.next(S.mrow))
                for h in range(2):
                    take(h)
                    for d in range(2):
                        last = mm(bank[h][:, d * SEQ:(d + 1) * SEQ], neg_one[:, d, :],
                                  MR[0:40, h, 1, :], start=True, stop=True, skip_group_check=True)
                    last.then_inc(S.wb_full, p.inc(S.wb_full))
                eng.wait_ge(S.kw, p.next(S.kw))
                eng.wait_ge(S.mv, p.next(S.mv))
                take(7)
                for h in range(2):
                    for d in range(2):
                        last = group(bank[7][DH * h:DH * h + DH, d * VW:(d + 1) * VW],
                                     [(KW[:, 2 * d + t, h, :], MV[:, 2 + t, h, :]) for t in range(2)])
                last.then_inc(S.st_full, p.inc(S.st_full))

                def scores(h):
                    take(4)
                    take(5)
                    r0 = DH * h
                    for t in range(2):
                        mm(bank[4][:, t * SEQ:(t + 1) * SEQ], MK[r0:r0 + DH, t * P:(t + 1) * P], MQ[r0:r0 + DH, :],
                           start=True, stop=True, skip_group_check=True)
                    for d in range(2):
                        last = mm(bank[5][:, d * SEQ:(d + 1) * SEQ], neg_one[:, d, :],
                                  MR[0:40, h, 0, :], start=True, stop=True, skip_group_check=True)
                    last.then_inc(S.nm_full, p.inc(S.nm_full))

                def sums(h):
                    eng.wait_ge(S.e_ready, p.next(S.e_ready))
                    take(6)
                    take(7)
                    r0 = DH * h
                    for d in range(2):
                        for t in range(2):
                            blocks = [(0, 0), (2, 1)][t:t + 1]
                            if (d, t) == (0, 1):
                                blocks = [(1, 0)] + blocks
                            if (d, t) == (1, 0):
                                blocks = [(1, 1)] + blocks
                            last = group(bank[6 + d][:, t * VW:(t + 1) * VW],
                                         [(QW[r0:r0 + DH, h, d, t * P:(t + 1) * P], C0[r0:r0 + DH, d, :])] +
                                         [(EE[:, h, 3 * d + b, :], MV[:, s, h, :]) for b, s in blocks])
                    last.then_inc(S.num_full, p.inc(S.num_full))

                scores(0)
                token_tiles(2, [(0, 0, toks(0)), (1, 0, toks(P))], (0, 1))
                scores(1)
                sums(0)
                eng.wait_ge(S.land[3], p.next(S.land[3], 16))
                take(2)
                group(bank[2][:, 0:SEQ], [(W[3][:, k, 0:P], UP[:, k, 0:SEQ]) for k in range(KD)]).then_inc(S.half[3], p.inc(S.half[3]))
                sums(1)
                take(3)
                group(bank[3][:, 0:SEQ], [(W[3][:, k, P:2 * P], UP[:, k, 0:SEQ]) for k in range(KD)]).then_inc(S.done[3], p.inc(S.done[3]))
                take(0)
                for h in range(2):
                    eng.wait_ge(S.hm, p.next(S.hm))
                    for t in range(2):
                        last = eng.transpose(bank[0][:, h * SEQ + t * P:h * SEQ + (t + 1) * P], HM[:, h, t, :], ident[:, :])
                last.then_inc(S.mt_full, p.inc(S.mt_full))

            def steps_f(r, d):
                eng.wait_ge(S.land[r], p.next(S.land[r], 16))
                for t in range(2):
                    b = 2 * (d % 2) + t
                    take(b)
                    for c, src in ((0, UP), (SEQ, U)):
                        for k in range(KD):
                            last = mm(bank[b][:, c:c + SEQ], W[r][:, k, t * P:(t + 1) * P],
                                      src[:, k, (0 if c == 0 else SEQ):(0 if c == 0 else SEQ) + SEQ],
                                      start=k == 0, stop=k == KD - 1, skip_group_check=True)
                            if c and k == KD - 1:
                                sem = S.done[r] if t else S.half[r]
                                last.then_inc(sem, p.inc(sem))
                            yield

            def steps_i(r):
                eng.wait_ge(S.land[r], p.next(S.land[r], 32))
                take(2)
                take(3)
                for n, (b, c, tok) in enumerate([(2, 0, perm(0)), (2, SW, perm(P)), (3, 0, toks(2 * P)), (3, SW, toks(3 * P))]):
                    for k in range(KD):
                        mm(bank[b][:, c:c + SW], tok(k), W[r][:, k, :], start=k == 0, stop=False, skip_group_check=True)
                        yield
                    last = mm(bank[b][:, c:c + SW], ones_row[0:1, 0:P], W[r][0:1, KD, :],
                              start=False, stop=True, skip_group_check=True)
                    if n == 3:
                        last.then_inc(S.done[r], p.inc(S.done[r]))
                    yield

            def weave(steps, n):
                for _ in range(n):
                    if next(steps, "end") == "end":
                        return

            def levels(d, steps):
                eng.wait_ge(S.kk, p.next(S.kk))
                take(4)
                for h in range(2):
                    for t in range(2):
                        last = mm(bank[4][:, (2 * h + t) * P:(2 * h + t + 1) * P], KK[:, d, h, t * P:(t + 1) * P],
                                  HQ[:, h, t * P:(t + 1) * P], start=True, stop=True, skip_group_check=True)
                last.then_inc(S.lev_full, p.inc(S.lev_full))
                weave(steps, 4)
                for lev in range(8):
                    b = 4 + (lev + 1) % 2
                    eng.wait_ge(S.lev_ready, p.next(S.lev_ready))
                    take(b)
                    for h in range(2):
                        if lev < 7:
                            for t in range(2):
                                last = mm(bank[b][:, (2 * h + t) * P:(2 * h + t + 1) * P],
                                          KL[lev % 2][:, h, t * P:(t + 1) * P], QL[lev % 2][:, h, t * P:(t + 1) * P],
                                          start=True, stop=True, skip_group_check=True)
                        else:
                            ks, qs = ((0, P), (P, 2 * P)) if d == 0 else ((P, 2 * P), (0, P))
                            last = mm(bank[b][:, h * P:(h + 1) * P], KL[lev % 2][:, h, ks[0]:ks[1]],
                                      QL[lev % 2][:, h, qs[0]:qs[1]], start=True, stop=True, skip_group_check=True)
                    last.then_inc(S.lev_full, p.inc(S.lev_full))
                    weave(steps, 4)
                eng.wait_ge(S.kc, p.next(S.kc))
                take(7)
                for h in range(2):
                    for t in range(2):
                        last = eng.transpose(bank[7][:, (2 * h + t) * P:(2 * h + t + 1) * P],
                                             KC[:, h, t * P:(t + 1) * P], ident[:, :])
                last.then_inc(S.kct_full, p.inc(S.kct_full))
                weave(steps, 1000)

            p.leave("recurrence")
            with p.loop(PAIRS) as i:
                slot_fm(0, lambda kk: UP[:, kk, 0:SEQ], SEQ)
                for _ in steps_f(1, 1):
                    pass
                eng.wait_ge(S.hq, p.next(S.hq))
                levels(0, steps_f(2, 0))
                levels(1, steps_i(3))
                eng.wait_ge(S.hi, p.next(S.hi))
                for d in range(2):
                    eng.wait_ge(S.kct, p.next(S.kct))
                    take(7)
                    for h in range(2):
                        last = group(bank[7][:, h * P:(h + 1) * P],
                                     [(KCT[:, d, 2 * h + t, :], HI[:, 2 + t, h * P:(h + 1) * P]) for t in range(2)])
                    last.then_inc(S.s0_full, p.inc(S.s0_full))
                eng.wait_ge(S.at, p.next(S.at, 2))
                eng.wait_ge(S.top, p.next(S.top, 2))
                eng.wait_ge(S.s0, p.next(S.s0, 2))
                eng.wait_ge(S.inter, p.next(S.inter, 2))
                take(6)
                first = True
                for h in range(2):
                    v0, v1 = HI[:, 0, h * P:(h + 1) * P], HI[:, 1, h * P:(h + 1) * P]
                    for d in range(2):
                        c = h * SEQ
                        ops = [(c, SEQ, S0[:, d, h, :], QR[:, d, h, :]), (c, P, v0, AT[:, d, 2 * h, :]),
                               (c + P, P, v1, AT[:, d, 2 * h + 1, :]),
                               (c + P, P, v0, A128[:, d, h, :]) if d == 0 else (c, P, v1, A128[:, d, h, :])]
                        for c0, n, x, y in ops:
                            last = mm(bank[6][:, c0:c0 + n], x, y, start=first, stop=h == 1 and d == 1 and y is ops[-1][3],
                                      skip_group_check=True)
                            first = False
                last.then_inc(S.o_full, p.inc(S.o_full))
                eng.wait_ge(S.osq, p.next(S.osq))
                take(7)
                mm(bank[7][:, :], mean_c[:, :], OSQ[:, :], start=True, stop=True).then_inc(S.omean, p.inc(S.omean))

            p.leave("merge")
            eng.wait_ge(S.hhd, p.next(S.hhd, PAIRS))
            with p.loop(PAIRS) as i:
                slot_fm(0, lambda kk: U[:, kk, 0:SEQ], SEQ)
                slot_fm(1, lambda kk: U[:, kk, 0:SEQ], SEQ)
                slot_fm(2, lambda kk: HMT[:, kk, :], SEQ)
                slot_fm(3, lambda kk: HHT[:, kk, :], SEQ)
            eng.wait_ge(S.mrg, p.next(S.mrg, KD))
            p.leave("output")
            for r in range(4):
                slot_fm(r, lambda kk: MRG[:, kk, :], SEQ)
            p.leave("feed")
            ffn(lambda kk: U[:, kk, 0:SEQ], SEQ, 0)
            stat(SQ, SEQ, True, KD)
            eng.wait_ge(S.u, p.next(S.u, KD))
            for t in range(2):
                for half in range(2):
                    b = 4 + 2 * t + half
                    take(b)
                    for k in range(4):
                        last = eng.transpose(bank[b][:, k * P:(k + 1) * P],
                                             U[:, 4 * half + k, t * P:(t + 1) * P], ident[:, :])
                    last.then_inc(S.tr_full, p.inc(S.tr_full))

        @block.scalar
        def _(eng):
            p = Count(eng, "act", S, rises)
            for b in range(8):
                p.skip(S.free[b])
            for r in range(SLOTS):
                p.skip(S.done[r])
            act = eng.activation
            eng.wait_ge(S.consts, p.next(S.consts))
            for n in range(10):
                p.skip(S.free[4 + n % 4])

            def rstd(b, n, dst, sem, eps=eps_rms, full=S.stat):
                eng.wait_ge(full, p.next(full))
                p.skip(S.free[b])
                act(LNT[:, 0:n], bank[b][:, 0:n], ACT.Ln, bias=eps[:, 0:1]).then_inc(S.order_act, p.inc(S.order_act))
                eng.wait_ge(S.order_act, p.now(S.order_act))
                ins = act(dst, LNT[:, 0:n], ACT.Exp, scale=-0.5)
                ins.then_inc(sem, p.inc(sem))
                eng.wait_ge(sem, p.now(sem))
                eng.sem_inc(S.free[b], 1)

            def squares(src, n, k0=0, k1=KD, sem=S.sq):
                for k in range(k0, k1):
                    act(SQ[:, k, 0:n], src(k), ACT.Square).then_inc(sem, p.inc(sem))

            def tile(r, t, fn, tiles=2, m=P):
                b = 2 * (r % 2) + t
                if t == tiles - 1:
                    eng.wait_ge(S.done[r], p.next(S.done[r]))
                else:
                    eng.wait_ge(S.half[r], p.next(S.half[r]))
                p.skip(S.free[b])
                fn(bank[b]).then_inc(S.free[b], 1)
                eng.wait_ge(S.free[b], p.now(S.free[b]))

            p.skip(S.free[6])
            eng.wait_ge(S.tr_done, p.next(S.tr_done, 11))
            act(CC[:, :, :], GS[:, 0, :, :], ACT.Silu).then_inc(S.cc, p.inc(S.cc))

            def ada_rows(r, b, parity):
                eng.wait_ge(S.done[r], p.next(S.done[r]))
                p.skip(S.free[b])
                act(AR[parity], bank[b][0:2, :].rearrange("p (a b) -> p a b", a=2), ACT.Copy).then_inc(S.ada_rows, p.inc(S.ada_rows))
                eng.wait_ge(S.ada_rows, p.now(S.ada_rows))
                eng.sem_inc(S.free[b], 1)

            def ada_columns(b, at):
                eng.wait_ge(S.ada_full, p.next(S.ada_full))
                p.skip(S.free[b])
                act(modf[:, bass.ds(at, 4), :] if not isinstance(at, int) else modf[:, at:at + 4, :],
                    bank[b][:, 0:8].rearrange("p (a b) -> p a b", a=4), ACT.Copy).then_inc(S.free[b], 1)
                eng.wait_ge(S.free[b], p.now(S.free[b]))

            with p.loop(LAYERS) as l:
                eng.wait_ge(S.par_ready, p.next(S.par_ready))
                p.skip(S.done[0])
                p.skip(S.free[4])
                squares(lambda k: H1[:, k, :], T1)
                rstd(4, T1, RS[:, 0:T1], S.rs)
                for t in range(2):
                    tile(1, t, lambda b: act(AV[:, t, :], b[:, 0:T1], ACT.Copy))
                for t in range(2):
                    tile(2, t, lambda b: act(AG[:, t, :], b[:, 0:T1], ACT.Sigmoid))
                act(LNT[:, 0:1], LNT[:, 0:1], ACT.Copy).then_inc(S.gate, p.inc(S.gate))
                eng.wait_ge(S.gate, p.now(S.gate))
                tile(3, 0, lambda b: act(FX[0:HEADS, :], b[0:HEADS, 0:T1], ACT.Identity, bias=PL[0:HEADS, C_BF:C_BF + 1]), tiles=1)
                act(FT[0:HEADS, :], FX[0:HEADS, :], ACT.Abs).then_inc(S.order_act, p.inc(S.order_act))
                eng.wait_ge(S.order_act, p.now(S.order_act))
                act(FT[0:HEADS, :], FT[0:HEADS, :], ACT.Exp, scale=-1.0).then_inc(S.order_act, p.inc(S.order_act))
                eng.wait_ge(S.order_act, p.now(S.order_act))
                act(FT[0:HEADS, :], FT[0:HEADS, :], ACT.Ln, bias=1.0).then_inc(S.f_act, p.inc(S.f_act))
                eng.wait_ge(S.f_act, p.now(S.f_act))
                for c, r in ((0, 0), (1, 1)):
                    for t in range(2):
                        tile(r, t, lambda b: act(QT[:, 2 * c + t, :], b[:, 0:T1], ACT.Copy, scale=DH ** -0.5))
                for c, r in ((0, 2), (1, 3)):
                    for t in range(2):
                        tile(r, t, lambda b: act(KT[:, 2 * c + t, :], b[:, 0:T1], ACT.Copy))
                for c, r in ((0, 0), (1, 1)):
                    eng.wait_ge(S.done[r], p.next(S.done[r]))
                    b0 = 2 * (r % 2)
                    cc = slice(c * SW, (c + 1) * SW)
                    act(V[:, 0, cc], bank[b0][:, 0:SW], ACT.Copy).then_inc(S.order_act, p.inc(S.order_act))
                    eng.wait_ge(S.order_act, p.now(S.order_act))
                    p.skip(S.free[b0])
                    p.skip(S.free[b0 + 1])
                    act(V[0:16, 2, cc], bank[b0][0:16, SW:2 * SW], ACT.Copy).then_inc(S.free[b0], 1)
                    act(V[:, 1, cc], bank[b0 + 1][:, 0:SW], ACT.Copy).then_inc(S.free[b0 + 1], 1)
                    act(LNT[:, 0:1], LNT[:, 0:1], ACT.Copy).then_inc(S.vt, p.inc(S.vt, 1))
                    eng.wait_ge(S.vt, p.now(S.vt))
                    act(LNT[:, 0:1], LNT[:, 0:1], ACT.Copy).then_inc(S.vt, p.inc(S.vt, 1))
                    eng.wait_ge(S.vt, p.now(S.vt))
                for t in range(2):
                    tile(2, t, lambda b: act(SCC[:, t, :], b[:, 0:T1], ACT.Copy))
                p.skip(S.free[6])
                for t in range(2):
                    tile(3, t, lambda b: act(SCX[:, t, :], b[:, 0:T1], ACT.Copy))
                eng.wait_ge(S.xc, p.next(S.xc, 2))
                for t in range(2):
                    act(SQ[:, t, 0:T1], CV[:, t, :], ACT.Square).then_inc(S.xcsq, p.inc(S.xcsq))
                rstd(7, T1, RS[:, 0:T1], S.cvrs, eps_ln, S.var)
                for t in range(2):
                    tile(0, t, lambda b: act(SCB[:, t, :], b[:, 0:T1], ACT.Copy))
                act(LNT[:, 0:1], LNT[:, 0:1], ACT.Copy).then_inc(S.sc_in, p.inc(S.sc_in))
                eng.wait_ge(S.sc_in, p.now(S.sc_in))
                for t in range(2):
                    eng.wait_ge(S.xn, p.next(S.xn))
                    act(CS[:, t, :], CV[:, t, :], ACT.Silu, bias=PL[:, C_LNB + t:C_LNB + t + 1]).then_inc(S.cact, p.inc(S.cact))
                for t in range(2):
                    tile(1, t, lambda b: act(YC[:, 4 + t, :], b[:, 0:T1], ACT.Copy))

                def exps(j):
                    h = j % 2
                    eng.wait_ge(S.s_ready, p.next(S.s_ready))
                    act(PR[h][:, 0:128], SC[h][:, 0:128], ACT.Exp, bias=NM[h][:, 0:1], accum_out=SM[h][:, 0:1])
                    act(PR[h][:, 128:384], SC[h][:, 128:384], ACT.Exp, bias=NM[h][:, 1:2], accum_out=SM[h][:, 1:2])
                    act(PR[h][0:16, 384:656], SC[h][0:16, 384:656], ACT.Exp, bias=NM[h][0:16, 2:3],
                               accum_out=SM[h][0:16, 2:3]).then_inc(S.p_exp, p.inc(S.p_exp))
                    p.skip(S.free[4 + h])
                    p.skip(S.free[6 + h])

                def evict(j):
                    h = j % 2
                    eng.wait_ge(S.pt_full, p.next(S.pt_full))
                    p.skip(S.free[h])
                    act(PT[h][:, 0:416], bank[h][:, 0:416], ACT.Copy).then_inc(S.order_act, p.inc(S.order_act))
                    eng.wait_ge(S.order_act, p.now(S.order_act))
                    act(PT[h][0:16, 416:432], bank[h][0:16, 416:432], ACT.Copy).then_inc(S.free[h], 1)
                    eng.wait_ge(S.free[h], p.now(S.free[h]))
                    act(LNT[:, 0:1], LNT[:, 0:1], ACT.Copy).then_inc(S.pt_ready, p.inc(S.pt_ready))
                    eng.wait_ge(S.pt_ready, p.now(S.pt_ready))
                    p.skip(S.done[(2 + 2 * j) % 4])
                    ada_rows((3 + 2 * j) % 4, ada_bank(j), h)
                    if h:
                        yb = 2 + (j // 2) % 2
                        eng.wait_ge(S.yt_full, p.next(S.yt_full))
                        p.skip(S.free[yb])
                        act(YC[:, j // 2, :], bank[yb][:, 0:T1], ACT.Copy).then_inc(S.free[yb], 1)
                        eng.wait_ge(S.free[yb], p.now(S.free[yb]))

                exps(0)
                for j in range(HEADS):
                    if j + 1 < HEADS:
                        exps(j + 1)
                    if j:
                        ada_columns(ada_bank(j - 1), l * 32 + 4 * (j - 1))
                    evict(j)
                ada_columns(ada_bank(HEADS - 1), l * 32 + 4 * (HEADS - 1))
                eng.wait_ge(S.ysc, p.next(S.ysc, 2))
                squares(lambda k: YC[:, k, :], T1, sem=S.hsq)
                for k in range(KD):
                    rstd(4 + k % 4, T1, RSH[:, k, :], S.hrs, full=S.hstat)

                for n, r in enumerate((2, 3, 0, 1)):
                    for t in range(2):
                        m = 2 * n + t

                        def both(b):
                            act(Y[:, m, :], b[:, 0:T1], ACT.Copy)
                            act(SQ[:, m, 0:T1], b[:, 0:T1], ACT.Square).then_inc(S.ysq, p.inc(S.ysq))
                            eng.wait_ge(S.ysq, p.now(S.ysq))
                            return act(LNT[:, 0:1], LNT[:, 0:1], ACT.Copy)
                        tile(r, t, both)
                rstd(4, T1, RS[:, 0:T1], S.rs)
                for k in range(KD):
                    eng.wait_ge(S.h_new, p.next(S.h_new))
                    act(SQ[:, k, 0:T1], H1[:, k, :], ACT.Square).then_inc(S.sq, p.inc(S.sq))
                rstd(4, T1, RS[:, 0:T1], S.rs)

                def up(g, r):
                    eng.wait_ge(S.z_used, p.next(S.z_used))
                    for s in range(2):
                        for t in range(2):
                            tile(r + s, t, lambda b: act(Z[:, g, 2 * s + t, :], b[:, 0:T1], ACT.Copy))
                            act(LNT[:, 0:1], LNT[:, 0:1], ACT.Copy).then_inc(S.z, p.inc(S.z))
                            eng.wait_ge(S.z, p.now(S.z))
                    eng.wait_ge(S.cg, p.next(S.cg))
                    act(SG[:, :, :], CZ[:, 0:2, :], ACT.Silu).then_inc(S.sg, p.inc(S.sg))

                with p.loop(5) as i:
                    up(0, 2)
                    up(1, 0)
                up(0, 2)
                with p.loop(2) as i:
                    for j in range(2):
                        p.skip(S.done[2 * j])
                        r = 2 * j + 1
                        for t in range(2):
                            sem = S.done[r] if t else S.half[r]
                            eng.wait_ge(sem, p.next(sem))
                            b = 2 * j + t
                            act(Y[:, bass.ds(i * 4 + (2 * j + t), 1), :].rearrange("p a b -> p (a b)"), bank[b][:, 0:T1], ACT.Copy)
                            act(SQ[:, bass.ds(i * 4 + (2 * j + t), 1), 0:T1].rearrange("p a b -> p (a b)"),
                                       bank[b][:, 0:T1], ACT.Square).then_inc(S.ysq, p.inc(S.ysq))
                            eng.wait_ge(S.ysq, p.now(S.ysq))
                            p.skip(S.free[b])
                            act(LNT[:, 0:1], LNT[:, 0:1], ACT.Copy).then_inc(S.free[b], 1)
                            eng.wait_ge(S.free[b], p.now(S.free[b]))
                rstd(4, T1, RS[:, 0:T1], S.rs)
                eng.wait_ge(S.h_new, p.next(S.h_new, KD))

            def mark(sem):
                act(LNT[:, 0:1], LNT[:, 0:1], ACT.Copy).then_inc(sem, p.inc(sem))
                eng.wait_ge(sem, p.now(sem))

            def col(c, i=None, n=1):
                return P2[:, c:c + n] if i is None else P2[:, bass.ds(i + c, n)]

            def free(b, ins):
                ins.then_inc(S.free[b], p.inc(S.free[b]))
                eng.wait_ge(S.free[b], p.now(S.free[b]))

            p.meet("second")
            p.skip(S.u, 2 * KD * LAYERS)
            p.skip(S.done[0])
            p.skip(S.free[4])
            eng.wait_ge(S.par2_ready, p.next(S.par2_ready))
            act(LBC[:, 2:4, :], LBC[:, 2:4, :], ACT.Exp).then_inc(S.sig, p.inc(S.sig))
            eng.wait_ge(S.sig, p.now(S.sig))
            for n, r in enumerate((2, 0)):
                p.skip(S.done[r - 1 if r else 3])
                ada_rows(r, n, 2 + n)
            for n in range(2):
                ada_columns(n, 64 + 4 * n)
            mark(S.mod_ready)
            p.meet("modulated")

            def norm(n, i_norm, shift):
                eng.wait_ge(S.x2_ready, p.next(S.x2_ready))
                squares(lambda k: H2[:, k, 0:n], n)
                rstd(4, n, RS[:, 0:n], S.rs)
                if shift is None:
                    return
                for k in range(KD):
                    eng.wait_ge(S.un, p.next(S.un))
                    for c in range(n // SEQ):
                        ins = act(U[:, k, c * SEQ:(c + 1) * SEQ], U[:, k, c * SEQ:(c + 1) * SEQ], ACT.Identity,
                                  bias=MOD[:, shift, k, c:c + 1])
                    ins.then_inc(S.u, p.inc(S.u))
                eng.wait_ge(S.u, p.now(S.u))

            def ffn(n, r0, i_norm, shift):
                norm(n, i_norm, shift)

                def group(g, r):
                    eng.wait_ge(S.sg2, p.next(S.sg2))
                    for t in range(2):
                        tile(r, t, lambda b: act(SG2[:, g, t, 0:n], b[:, 0:n], ACT.Silu))
                    r = (r + 1) % 4
                    p.skip(S.half[r])
                    p.skip(S.done[r])
                    p.skip(S.free[2 * (r % 2)])
                    p.skip(S.free[2 * (r % 2) + 1])

                with p.loop(5) as i:
                    group(0, r0)
                    group(1, (r0 + 2) % 4)
                group(0, r0)
                with p.loop(2) as i:
                    for j in range(2):
                        r = (r0 + 2 + 2 * j) % 4
                        p.skip(S.done[r])
                        r = (r + 1) % 4
                        p.skip(S.half[r])
                        p.skip(S.done[r])
                        p.skip(S.free[2 * j])
                        p.skip(S.free[2 * j + 1])

            ffn(2 * SEQ, 1, 0, 0)
            norm(2 * SEQ, 1, 3)

            p.meet("gates")
            rows = [slice(32 * d, 32 * d + HEADS) for d in range(2)]
            eng.wait_ge(S.done[3], p.next(S.done[3]))
            for g, dst in enumerate((GI, GF)):
                for d in range(2):
                    ins = act(dst[rows[d], :], bank[g][rows[d], :], ACT.Identity, bias=P2[rows[d], B_IF + g:B_IF + g + 1])
                ins.then_inc(S.free[g], p.inc(S.free[g]))
                eng.wait_ge(S.free[g], p.now(S.free[g]))
            for fn, src, kw in ((ACT.Abs, GF, {}), (ACT.Exp, GT_, dict(scale=-1.0)), (ACT.Ln, GT_, dict(bias=1.0))):
                for d in range(2):
                    ins = act(GT_[rows[d], :], src[rows[d], :], fn, **kw)
                sem = S.gate_in if fn is ACT.Ln else S.order_act
                ins.then_inc(sem, p.inc(sem))
                eng.wait_ge(sem, p.now(sem))
            eng.wait_ge(S.gate_m, p.next(S.gate_m))
            for d in range(2):
                act(G4[rows[d], 1, :], GI[rows[d], SEQ:2 * SEQ], ACT.Exp, bias=G1[rows[d], 1:2])
                act(G4[rows[d], 2, :], GM[rows[d], :], ACT.Exp, scale=-1.0, bias=G1[rows[d], 2:3])
                ins = act(G4[rows[d], 3, :], GT_[rows[d], 0:SEQ], ACT.Exp, scale=-1.0)
            ins.then_inc(S.gate_exp, p.inc(S.gate_exp))
            eng.wait_ge(S.gate_exp, p.now(S.gate_exp))

            p.meet("memory")
            with p.loop(PAIRS) as i:
                eng.wait_ge(S.done[0], p.next(S.done[0]))
                act(MQ, bank[0][:, 0:SEQ], ACT.Identity, scale=DH ** -0.5, bias=MQB[:, bass.ds(i, 1)])
                act(MK, bank[0][:, SEQ:2 * SEQ], ACT.Identity, bias=col(B_MK, i)).then_inc(S.free[0], p.inc(S.free[0]))
                eng.wait_ge(S.free[0], p.now(S.free[0]))
                act(MKC[:, :, :], bank[1][:, 0:SEQ].rearrange("p (a b) -> p a b", a=2), ACT.Copy).then_inc(S.free[1], p.inc(S.free[1]))
                eng.wait_ge(S.free[1], p.now(S.free[1]))
                eng.wait_ge(S.done[1], p.next(S.done[1]))
                for n in range(2):
                    for h in range(2):
                        ins = act(MV[:, 2 * n:2 * n + 2, h, 0:P],
                                  bank[2 + n][:, :].rearrange("p (a b c) -> p a b c", a=2, b=2)[:, :, h, :], ACT.Copy)
                    ins.then_inc(S.free[2 + n], p.inc(S.free[2 + n]))
                    eng.wait_ge(S.free[2 + n], p.now(S.free[2 + n]))
                mark(S.mv)
                p.skip(S.free[0])
                p.skip(S.free[1])
                eng.wait_ge(S.st_full, p.next(S.st_full))
                act(C0[:, :, :], bank[7][:, 0:2 * VW].rearrange("p (a b) -> p a b", a=2), ACT.Copy).then_inc(S.free[7], p.inc(S.free[7]))
                eng.wait_ge(S.free[7], p.now(S.free[7]))

                def exps(h):
                    eng.wait_ge(S.free[5], p.next(S.free[5]))
                    act(EE[:, h, :, :], EE[:, h, :, :], ACT.Exp).then_inc(S.e_exp, p.inc(S.e_exp))
                    eng.wait_ge(S.e_exp, p.now(S.e_exp))
                    p.skip(S.free[4])

                def stats(h):
                    eng.wait_ge(S.hs, p.next(S.hs))
                    for t in range(2):
                        act(LNT[:, 0:P], HS[:, h, t, :], ACT.Square, accum_out=SS[:, h, t:t + 1]).then_inc(S.order_act, p.inc(S.order_act))
                        eng.wait_ge(S.order_act, p.now(S.order_act))
                    act(SS[:, h, :], SS[:, h, :], ACT.Ln, scale=1.0 / P, bias=eps_rms[:, 0:1]).then_inc(S.order_act, p.inc(S.order_act))
                    eng.wait_ge(S.order_act, p.now(S.order_act))
                    act(RR[:, h, :], SS[:, h, :], ACT.Exp, scale=-0.5).then_inc(S.mrs, p.inc(S.mrs))
                    eng.wait_ge(S.mrs, p.now(S.mrs))

                def gate(t):
                    sem = S.done[3] if t else S.half[3]
                    eng.wait_ge(sem, p.next(sem))
                    act(HG[:, bass.ds(i * 2 + t, 1), :].rearrange("p a b -> p (a b)"), bank[2 + t][:, 0:SEQ],
                                    ACT.Silu, bias=col(B_HGATE + t, i * 2)).then_inc(S.free[2 + t], p.inc(S.free[2 + t]))
                    eng.wait_ge(S.free[2 + t], p.now(S.free[2 + t]))

                exps(0)
                eng.wait_ge(S.done[2], p.next(S.done[2]))
                for t in range(2):
                    act(MO[:, t, :], bank[t][:, 0:SEQ], ACT.Sigmoid).then_inc(S.free[t], p.inc(S.free[t]))
                    eng.wait_ge(S.free[t], p.now(S.free[t]))
                exps(1)
                gate(0)
                for h in range(2):
                    p.skip(S.free[6])
                    p.skip(S.free[7])
                    stats(h)
                gate(1)
                eng.wait_ge(S.mt_full, p.next(S.mt_full))
                for h in range(2):
                    ins = act(HMT[:, bass.ds(i * 2 + h, 1), :].rearrange("p a b -> p (a b)"), bank[0][:, h * SEQ:(h + 1) * SEQ],
                              ACT.Copy, scale=col(B_ML + h, i * 2))
                ins.then_inc(S.free[0], p.inc(S.free[0]))
                eng.wait_ge(S.free[0], p.now(S.free[0]))

            p.meet("recurrence")
            with p.loop(PAIRS) as i:
                for t in range(2):
                    tile(0, t, lambda b: act(HQ[:, t, :], b[:, 0:SEQ], ACT.Silu, bias=col(B_HQ + t, i * 2)))
                mark(S.hq)

                def forget(d, r, b0):
                    for t in range(2):
                        sem = S.done[r] if t else S.half[r]
                        eng.wait_ge(sem, p.next(sem))
                        act(FF_[:, d, t, :], bank[b0 + t][:, :], ACT.Sigmoid, bias=col(B_HF + 8 * d + t, i * 2))
                        act(KK[:, d, t, :], bank[b0 + t][:, :], ACT.Sigmoid, scale=-1.0,
                                         bias=NB[:, bass.ds(i * 2 + (8 * d + t), 1)]).then_inc(S.free[b0 + t], p.inc(S.free[b0 + t]))
                        eng.wait_ge(S.free[b0 + t], p.now(S.free[b0 + t]))

                def tops(d):
                    eng.wait_ge(S.lev_full, p.next(S.lev_full, 9))
                    p.skip(S.free[4], 4)
                    p.skip(S.free[5], 4)
                    act(A128[:, d, :, :], bank[4][:, 0:SEQ].rearrange("p (a b) -> p a b", a=2), ACT.Copy).then_inc(S.free[4], p.inc(S.free[4]))
                    eng.wait_ge(S.free[4], p.now(S.free[4]))
                    mark(S.top)
                    eng.wait_ge(S.kct_full, p.next(S.kct_full))
                    act(KCT[:, d, :, :], bank[7][:, :].rearrange("p (a b) -> p a b", a=4), ACT.Copy).then_inc(S.free[7], p.inc(S.free[7]))
                    eng.wait_ge(S.free[7], p.now(S.free[7]))
                    mark(S.kct)

                forget(0, 1, 2)
                tops(0)
                forget(1, 2, 0)
                tops(1)
                eng.wait_ge(S.done[3], p.next(S.done[3]))
                for n in range(2):
                    act(HI[:, 2 * n:2 * n + 2, :], bank[2 + n][:, :].rearrange("p (a b) -> p a b", a=2), ACT.Copy).then_inc(S.free[2 + n], p.inc(S.free[2 + n]))
                    eng.wait_ge(S.free[2 + n], p.now(S.free[2 + n]))
                mark(S.hi)
                for d in range(2):
                    eng.wait_ge(S.s0_full, p.next(S.s0_full))
                    act(S0[:, d, :, :], bank[7][:, 0:SEQ].rearrange("p (a b) -> p a b", a=2), ACT.Copy).then_inc(S.free[7], p.inc(S.free[7]))
                    eng.wait_ge(S.free[7], p.now(S.free[7]))
                    mark(S.s0)
                eng.wait_ge(S.o_full, p.next(S.o_full))
                act(OSQ, bank[6][:, :], ACT.Square).then_inc(S.osq, p.inc(S.osq))
                eng.wait_ge(S.osq, p.now(S.osq))
                p.skip(S.free[6])
                eng.wait_ge(S.omean, p.next(S.omean))
                act(LNT[:, :], bank[7][:, :], ACT.Ln, scale=2.0, bias=eps_rms[:, 0:1]).then_inc(S.free[7], p.inc(S.free[7]))
                eng.wait_ge(S.free[7], p.now(S.free[7]))
                act(RS[:, :], LNT[:, :], ACT.Exp, scale=-0.5).then_inc(S.ors, p.inc(S.ors))
                eng.wait_ge(S.ors, p.now(S.ors))

            gms, ghs = HQ, HI[:, 0:2, :]
            p.meet("merge")
            with p.loop(PAIRS) as i:
                for r, dst, c in ((0, gms, B_GM), (1, ghs, B_GH)):
                    for t in range(2):
                        tile(r, t, lambda b: act(dst[:, t, :], b[:, 0:SEQ], ACT.Sigmoid, bias=col(c + t, i * 2)))
                for r in (2, 3):
                    p.skip(S.half[r])
                    p.skip(S.done[r])
                for b in range(4):
                    p.skip(S.free[b])
                eng.wait_ge(S.mrg, p.next(S.mrg, 2))
            p.meet("feed")
            ffn(SEQ, 0, 2, 6)
            norm(SEQ, None, None)

        @block.vector
        def _(eng):
            p = Count(eng, "dve", S, rises)
            for b in range(8):
                p.skip(S.free[b])
            p.skip(S.done[0])
            stt, tt, ts = eng.scalar_tensor_tensor, eng.tensor_tensor, eng.tensor_scalar
            for g in range(2):
                eng.memset(CX[:, :, 0:2], 0.0).then_inc(S.z_used, p.inc(S.z_used))
                eng.wait_ge(S.z_used, p.now(S.z_used))
            eng.wait_ge(S.consts, p.next(S.consts))
            spans = [(H1, 0, P), (H1, P, P), (H1, 2 * P, META), (H2, SEQ, P), (H2, SEQ + P, P)]
            for n, (t, half) in enumerate((t, half) for t in range(5) for half in range(2)):
                b = 4 + n % 4
                dst, c, w = spans[t]
                eng.wait_ge(S.tr_full, p.next(S.tr_full))
                p.skip(S.free[b])
                eng.tensor_copy(dst[:, 4 * half:4 * half + 4, c:c + w],
                                bank[b][:, 0:4 * w].rearrange("p (a b) -> p a b", a=4)).then_inc(S.free[b], 1)
                eng.wait_ge(S.free[b], p.now(S.free[b]))
                eng.memset(CX[:, 0, 0:2], 0.0).then_inc(S.tr_done, p.inc(S.tr_done))
                eng.wait_ge(S.tr_done, p.now(S.tr_done))
            eng.wait_ge(S.tr_full, p.next(S.tr_full))
            p.skip(S.free[6])
            eng.tensor_copy(GS[:, 0, :, :], bank[6][:, 0:2 * KD].rearrange("p (c k) -> p k c", c=2)).then_inc(S.free[6], 1)
            eng.wait_ge(S.free[6], p.now(S.free[6]))
            eng.memset(CX[:, 0, 0:2], 0.0).then_inc(S.tr_done, p.inc(S.tr_done))
            eng.wait_ge(S.tr_done, p.now(S.tr_done))
            eng.wait_ge(S.consts, p.next(S.consts))

            def par(c):
                return PL[:, c:c + 1]

            def scale(src, c, n, dst):
                eng.wait_ge(S.rs, p.next(S.rs))
                for k in range(KD):
                    stt(dst(k), src(k), par(c + k), RS[:, 0:n], ALU.mult, ALU.mult).then_inc(S.u, p.inc(S.u))

            def residual(c):
                eng.wait_ge(S.rs, p.next(S.rs))
                for k in range(KD):
                    stt(Y[:, k, :], Y[:, k, :], par(c + k), RS[:, 0:T1], ALU.mult, ALU.mult).then_inc(S.order_dve, p.inc(S.order_dve))
                    eng.wait_ge(S.order_dve, p.now(S.order_dve))
                    tt(H1[:, k, :], H1[:, k, :], Y[:, k, :], ALU.add).then_inc(S.h_new, p.inc(S.h_new))
                eng.wait_ge(S.h_new, p.now(S.h_new))

            with p.loop(LAYERS) as l:
                eng.wait_ge(S.done[0], p.next(S.done[0]))
                p.skip(S.done[0], 15)
                p.skip(S.free[4])
                eng.tensor_copy(PL[:, 0:C_BF], bank[4][:, 0:C_BF]).then_inc(S.order_dve, p.inc(S.order_dve))
                eng.wait_ge(S.order_dve, p.now(S.order_dve))
                eng.tensor_copy(PL[0:HEADS, C_BF:NPAR], bank[4][0:HEADS, C_BF:NPAR]).then_inc(S.free[4], 1)
                eng.wait_ge(S.free[4], p.now(S.free[4]))
                eng.memset(AP_[:, :, 0:TAPS - 1], 0.0).then_inc(S.order_dve, p.inc(S.order_dve))
                eng.wait_ge(S.order_dve, p.now(S.order_dve))
                eng.memset(CX[:, :, 0:2], 0.0).then_inc(S.par_ready, p.inc(S.par_ready))
                eng.wait_ge(S.par_ready, p.now(S.par_ready))
                p.skip(S.free[4])
                scale(lambda k: H1[:, k, :], C_PRE, T1, lambda k: U[:, k, 0:T1])
                eng.wait_ge(S.gate, p.next(S.gate))
                for t in range(2):
                    tt(AP_[:, t, TAPS - 1:], AV[:, t, :], AG[:, t, :], ALU.mult).then_inc(S.order_dve, p.inc(S.order_dve))
                    eng.wait_ge(S.order_dve, p.now(S.order_dve))
                for b in (2, 3, 0, 1, 2):
                    p.skip(S.free[b])
                for tap in range(TAPS):
                    for t in range(2):
                        w = par(C_DW + 2 * tap + t)
                        src = AP_[:, t, tap:tap + T1]
                        if tap == 0:
                            ins = ts(CV[:, t, :], src, w, par(C_DWB + t), ALU.mult, ALU.add)
                        else:
                            ins = stt(CV[:, t, :], src, w, CV[:, t, :], ALU.mult, ALU.add)
                        if tap == TAPS - 1:
                            ins.then_inc(S.conv, p.inc(S.conv))
                        elif t:
                            ins.then_inc(S.order_dve, p.inc(S.order_dve))
                            eng.wait_ge(S.order_dve, p.now(S.order_dve))
                eng.wait_ge(S.conv, p.now(S.conv))
                eng.wait_ge(S.f_act, p.next(S.f_act))
                ts(FM[0:HEADS, :], FX[0:HEADS, :], 0.0, None, ALU.min).then_inc(S.order_dve, p.inc(S.order_dve))
                eng.wait_ge(S.order_dve, p.now(S.order_dve))
                tt(FM[0:HEADS, :], FM[0:HEADS, :], FT[0:HEADS, :], ALU.subtract).then_inc(S.order_dve, p.inc(S.order_dve))
                eng.wait_ge(S.order_dve, p.now(S.order_dve))
                eng.tensor_tensor_scan(FC[0:HEADS, :], ones_row[0:HEADS, 0:T1], FM[0:HEADS, :], 0.0, ALU.mult, ALU.add).then_inc(S.f_ready, p.inc(S.f_ready))
                eng.wait_ge(S.f_ready, p.now(S.f_ready))
                for b in (0, 1, 2, 3, 0, 1, 2, 3, 0, 1, 2, 3, 0, 1):
                    p.skip(S.free[b])
                eng.wait_ge(S.mean, p.next(S.mean))
                p.skip(S.free[6])
                for t in range(2):
                    tt(CV[:, t, :], CV[:, t, :], bank[6][:, 0:T1], ALU.subtract).then_inc(S.xc, p.inc(S.xc))
                    eng.wait_ge(S.xc, p.now(S.xc))
                eng.memset(tick[:, 0:1], 0.0).then_inc(S.free[6], 1)
                eng.wait_ge(S.free[6], p.now(S.free[6]))
                for b in (2, 3, 7, 0, 1, 2, 3):
                    p.skip(S.free[b])
                eng.wait_ge(S.cvrs, p.next(S.cvrs))
                for t in range(2):
                    stt(CV[:, t, :], CV[:, t, :], par(C_LNG + t), RS[:, 0:T1], ALU.mult, ALU.mult).then_inc(S.xn, p.inc(S.xn))
                    eng.wait_ge(S.xn, p.now(S.xn))
                eng.wait_ge(S.sc_in, p.next(S.sc_in))
                for t in range(2):
                    tt(CX[:, t, 2:], SCC[:, t, :], SCX[:, t, :], ALU.mult).then_inc(S.order_dve, p.inc(S.order_dve))
                    eng.wait_ge(S.order_dve, p.now(S.order_dve))
                for t in range(2):
                    ts(SCC[:, t, :], CX[:, t, 0:T1], par(C_SC + t), None, ALU.mult).then_inc(S.order_dve, p.inc(S.order_dve))
                    eng.wait_ge(S.order_dve, p.now(S.order_dve))
                    for tap in (1, 2):
                        stt(SCC[:, t, :], CX[:, t, tap:tap + T1], par(C_SC + 2 * tap + t), SCC[:, t, :], ALU.mult, ALU.add).then_inc(S.order_dve, p.inc(S.order_dve))
                        eng.wait_ge(S.order_dve, p.now(S.order_dve))
                    tt(YC[:, 6 + t, :], SCC[:, t, :], SCB[:, t, :], ALU.mult).then_inc(S.ysc, p.inc(S.ysc))
                    eng.wait_ge(S.ysc, p.now(S.ysc))

                def mask_max(j):
                    h = j % 2
                    ba, bb = 4 + h, 6 + h
                    eng.wait_ge(S.s_full, p.next(S.s_full))
                    p.skip(S.free[ba])
                    p.skip(S.free[bb])
                    tt(SC[h][:, 0:384], bank[ba][:, 0:384], mask01[:, :], ALU.add).then_inc(S.free[ba], 1)
                    tt(SC[h][0:16, 384:656], bank[bb][0:16, 0:T1], mask2[:, :], ALU.add).then_inc(S.free[bb], 1)
                    eng.wait_ge(S.free[ba], p.now(S.free[ba]))
                    eng.wait_ge(S.free[bb], p.now(S.free[bb]))
                    eng.tensor_reduce(MX[h][:, 0:1], SC[h][:, 0:128], AX_X, ALU.max)
                    eng.tensor_reduce(MX[h][:, 1:2], SC[h][:, 128:384], AX_X, ALU.max)
                    eng.tensor_reduce(MX[h][0:16, 2:3], SC[h][0:16, 384:656], AX_X, ALU.max).then_inc(S.order_dve, p.inc(S.order_dve))
                    eng.wait_ge(S.order_dve, p.now(S.order_dve))
                    ts(NM[h][:, 0:2], MX[h][:, 0:2], -1.0, None, ALU.mult)
                    ts(NM[h][0:16, 2:3], MX[h][0:16, 2:3], -1.0, None, ALU.mult).then_inc(S.s_ready, p.inc(S.s_ready))
                    eng.wait_ge(S.s_ready, p.now(S.s_ready))

                def normalise(j):
                    h = j % 2
                    eng.wait_ge(S.p_exp, p.next(S.p_exp))
                    eng.reciprocal(RC[h][:, 0:2], SM[h][:, 0:2])
                    eng.reciprocal(RC[h][0:16, 2:3], SM[h][0:16, 2:3]).then_inc(S.order_dve, p.inc(S.order_dve))
                    eng.wait_ge(S.order_dve, p.now(S.order_dve))
                    ts(PR[h][:, 0:128], PR[h][:, 0:128], RC[h][:, 0:1], None, ALU.mult)
                    ts(PR[h][:, 128:384], PR[h][:, 128:384], RC[h][:, 1:2], None, ALU.mult)
                    ts(PR[h][0:16, 384:656], PR[h][0:16, 384:656], RC[h][0:16, 2:3], None, ALU.mult).then_inc(S.p_norm, p.inc(S.p_norm))
                    eng.wait_ge(S.p_norm, p.now(S.p_norm))

                mask_max(0)
                for j in range(HEADS):
                    if j + 1 < HEADS:
                        mask_max(j + 1)
                    normalise(j)
                for k in range(KD):
                    eng.wait_ge(S.hrs, p.next(S.hrs))
                    p.skip(S.free[4 + k % 4])
                    stt(RSH[:, k, :], YC[:, k, :], par(C_HEAD + k), RSH[:, k, :], ALU.mult, ALU.mult).then_inc(S.yh, p.inc(S.yh))
                residual(C_POST)
                p.skip(S.free[4], 2)
                scale(lambda k: H1[:, k, :], C_FPRE, T1, lambda k: U[:, k, 0:T1])

                def up(g, n):
                    for i in range(4):
                        eng.wait_ge(S.z, p.next(S.z))
                        z = Z[:, g, i, :]
                        c = C_FC + (i // 2) * KF + (i % 2)

                        def w(tap):
                            return PL[:, bass.ds(n * 2 + (c + tap * 2 * KF), 1)]
                        ts(CZ[:, i, :], z, w(2), None, ALU.mult).then_inc(S.order_dve, p.inc(S.order_dve))
                        eng.wait_ge(S.order_dve, p.now(S.order_dve))
                        stt(CZ[:, i, 1:], Z[:, g, i, 0:T1 - 1], w(1), CZ[:, i, 1:], ALU.mult, ALU.add).then_inc(S.order_dve, p.inc(S.order_dve))
                        eng.wait_ge(S.order_dve, p.now(S.order_dve))
                        sem = S.cg if i == 1 else S.z_used if i == 3 else S.order_dve
                        stt(CZ[:, i, 2:], Z[:, g, i, 0:T1 - 2], w(0), CZ[:, i, 2:], ALU.mult, ALU.add).then_inc(sem, p.inc(sem))
                        eng.wait_ge(sem, p.now(sem))
                    eng.wait_ge(S.sg, p.next(S.sg))
                    tt(HID[:, bass.ds(n * 2, 2), :], SG[:, :, :], CZ[:, 2:4, :], ALU.mult).then_inc(S.hid, p.inc(S.hid))
                    eng.wait_ge(S.hid, p.now(S.hid))

                with p.loop(5) as i:
                    up(0, i * 2)
                    up(1, i * 2 + 1)
                up(0, 10)
                p.skip(S.free[4])
                residual(C_FPOST)
            def free(b, ins):
                ins.then_inc(S.free[b], p.inc(S.free[b]))
                eng.wait_ge(S.free[b], p.now(S.free[b]))

            def flat(v):
                return v.rearrange("p a b -> p (a b)")

            p.meet("second")
            eng.wait_ge(S.consts, p.next(S.consts))
            eng.wait_ge(S.done[0], p.next(S.done[0]))
            eng.tensor_copy(P2[:, 0:B_IF], bank[4][:, 0:B_IF]).then_inc(S.order_dve, p.inc(S.order_dve))
            eng.wait_ge(S.order_dve, p.now(S.order_dve))
            eng.tensor_copy(P2[0:HEADS, B_IF:NPAR2], bank[4][0:HEADS, B_IF:NPAR2]).then_inc(S.order_dve, p.inc(S.order_dve))
            eng.wait_ge(S.order_dve, p.now(S.order_dve))
            eng.tensor_copy(P2[32:32 + HEADS, B_IF:NPAR2], bank[4][32:32 + HEADS, B_IF:NPAR2]).then_inc(S.free[4], p.inc(S.free[4]))
            eng.wait_ge(S.free[4], p.now(S.free[4]))
            L = P2[:, B_LB:B_LB + 32].rearrange("p (d j t) -> p d j t", d=2, j=2)
            lv = LBC[:, :, :].rearrange("p q (d t) -> p q d t", d=2)
            tt(lv[:, 0], L[:, :, 0, :], L[:, :, 1, :], ALU.max).then_inc(S.order_dve, p.inc(S.order_dve))
            eng.wait_ge(S.order_dve, p.now(S.order_dve))
            tt(lv[:, 2], L[:, :, 0, :], lv[:, 0], ALU.subtract).then_inc(S.order_dve, p.inc(S.order_dve))
            eng.wait_ge(S.order_dve, p.now(S.order_dve))
            tt(lv[:, 3], L[:, :, 1, :], lv[:, 0], ALU.subtract).then_inc(S.order_dve, p.inc(S.order_dve))
            eng.wait_ge(S.order_dve, p.now(S.order_dve))
            ts(NB[:, :], P2[:, B_HF:B_HF + 16], -1.0, None, ALU.mult).then_inc(S.order_dve, p.inc(S.order_dve))
            eng.wait_ge(S.order_dve, p.now(S.order_dve))
            ts(MQB[:, :], P2[:, B_MQ:B_MQ + 4], DH ** -0.5, None, ALU.mult).then_inc(S.par2_ready, p.inc(S.par2_ready))
            eng.wait_ge(S.par2_ready, p.now(S.par2_ready))
            eng.wait_ge(S.sig, p.next(S.sig))
            tt(LBC[:, 1, :], LBC[:, 2, :], LBC[:, 3, :], ALU.add).then_inc(S.order_dve, p.inc(S.order_dve))
            eng.wait_ge(S.order_dve, p.now(S.order_dve))
            eng.reciprocal(LBC[:, 1, :], LBC[:, 1, :]).then_inc(S.order_dve, p.inc(S.order_dve))
            eng.wait_ge(S.order_dve, p.now(S.order_dve))
            tt(LBC[:, 0, :], LBC[:, 2, :], LBC[:, 1, :], ALU.mult).then_inc(S.order_dve, p.inc(S.order_dve))
            eng.wait_ge(S.order_dve, p.now(S.order_dve))
            ts(LBC[:, 1, :], LBC[:, 0, :], -1.0, 1.0, ALU.mult, ALU.add).then_inc(S.order_dve, p.inc(S.order_dve))
            eng.wait_ge(S.order_dve, p.now(S.order_dve))
            eng.tensor_copy(H2[:, :, 0:SEQ], H1[:, :, META:T1]).then_inc(S.order_dve, p.inc(S.order_dve))
            eng.wait_ge(S.order_dve, p.now(S.order_dve))
            p.meet("modulated")
            eng.wait_ge(S.mod_ready, p.next(S.mod_ready))
            tt(modf, modf, P2[:, B_ADA:B_ADA + NMOD * KD].unsqueeze(2).to_broadcast([P, NMOD * KD, 2]), ALU.add).then_inc(S.order_dve, p.inc(S.order_dve))
            eng.wait_ge(S.order_dve, p.now(S.order_dve))
            for n, (gain, sc) in enumerate(((B_N1, 1), (B_N2, 4), (B_N3, 7))):
                ts(GS[:, n], MOD[:, sc], 1.0, None, ALU.add).then_inc(S.order_dve, p.inc(S.order_dve))
                eng.wait_ge(S.order_dve, p.now(S.order_dve))
                tt(GS[:, n], GS[:, n], P2[:, gain:gain + KD].unsqueeze(2).to_broadcast([P, KD, 2]), ALU.mult).then_inc(S.order_dve, p.inc(S.order_dve))
                eng.wait_ge(S.order_dve, p.now(S.order_dve))
            for n, (g, f) in enumerate(((2, 0.5), (5, 1.0), (8, 0.5))):
                ts(GATE[:, n], MOD[:, g], f, None, ALU.mult).then_inc(S.order_dve, p.inc(S.order_dve))
                eng.wait_ge(S.order_dve, p.now(S.order_dve))
            for g in range(2):
                eng.memset(tick[:, 0:1], 0.0).then_inc(S.sg2, p.inc(S.sg2))
                eng.wait_ge(S.sg2, p.now(S.sg2))
            gatef = GATE[:, :, :, :].rearrange("p a b c -> p (a b c)")
            eng.memset(tick[:, 0:1], 0.0).then_inc(S.x2_ready, p.inc(S.x2_ready))
            eng.wait_ge(S.x2_ready, p.now(S.x2_ready))

            def norm(n, i_norm):
                eng.wait_ge(S.rs, p.next(S.rs))
                p.skip(S.free[4])
                for k in range(KD):
                    for c in range(n // SEQ):
                        cc = slice(c * SEQ, (c + 1) * SEQ)
                        ins = stt(U[:, k, cc], H2[:, k, cc], GS[:, i_norm, k, c:c + 1], RS[:, cc], ALU.mult, ALU.mult)
                    ins.then_inc(S.un, p.inc(S.un))

            def ffn(n, r0, i_norm):
                norm(n, i_norm)
                p.skip(S.u, KD)

                def group(g, r, m):
                    p.skip(S.half[r])
                    p.skip(S.done[r])
                    for t in range(2):
                        eng.wait_ge(S.free[2 * (r % 2) + t], p.next(S.free[2 * (r % 2) + t]))
                    r = (r + 1) % 4
                    for t in range(2):
                        b = 2 * (r % 2) + t
                        sem = S.done[r] if t else S.half[r]
                        eng.wait_ge(sem, p.next(sem))
                        tt(flat(HID2[:, bass.ds(m + t, 1), 0:n]), SG2[:, g, t, 0:n], bank[b][:, 0:n], ALU.mult).then_inc(S.free[b], p.inc(S.free[b]))
                        eng.wait_ge(S.free[b], p.now(S.free[b]))
                    eng.memset(tick[:, 0:1], 0.0).then_inc(S.hid, p.inc(S.hid))
                    eng.wait_ge(S.hid, p.now(S.hid))
                    eng.memset(tick[:, 0:1], 0.0).then_inc(S.sg2, p.inc(S.sg2))
                    eng.wait_ge(S.sg2, p.now(S.sg2))

                with p.loop(5) as i:
                    group(0, r0, i * 4)
                    group(1, (r0 + 2) % 4, i * 4 + 2)
                group(0, r0, 20)
                with p.loop(2) as i:
                    for j in range(2):
                        r = (r0 + 2 + 2 * j) % 4
                        p.skip(S.done[r])
                        r = (r + 1) % 4
                        for t in range(2):
                            b = 2 * j + t
                            sem = S.done[r] if t else S.half[r]
                            eng.wait_ge(sem, p.next(sem))
                            for c in range(n // SEQ):
                                x = flat(H2[:, bass.ds(i * 4 + (2 * j + t), 1), c * SEQ:(c + 1) * SEQ])
                                ins = stt(x, bank[b][:, c * SEQ:(c + 1) * SEQ],
                                          gatef[:, bass.ds(i * 8 + (4 * j + 2 * t + 16 * i_norm + c), 1)],
                                          x, ALU.mult, ALU.add)
                            ins.then_inc(S.free[b], p.inc(S.free[b]))
                            eng.wait_ge(S.free[b], p.now(S.free[b]))
                eng.memset(tick[:, 0:1], 0.0).then_inc(S.x2_ready, p.inc(S.x2_ready))
                eng.wait_ge(S.x2_ready, p.now(S.x2_ready))

            ffn(2 * SEQ, 1, 0)
            norm(2 * SEQ, 1)
            for k in range(KD):
                eng.wait_ge(S.u, p.next(S.u))
                eng.tensor_copy(UP[:, k, 0:SEQ].rearrange("p (c r) -> p r c", r=4),
                                       U[:, k, 0:SEQ].rearrange("p (r c) -> p r c", r=4)).then_inc(S.up, p.inc(S.up))
            eng.wait_ge(S.up, p.now(S.up))

            rows = [slice(32 * d, 32 * d + HEADS) for d in range(2)]
            scan = eng.tensor_tensor_scan
            p.meet("gates")
            for v in (GM, G4[:, :, :]):
                eng.memset(v[0:40], 0.0).then_inc(S.order_dve, p.inc(S.order_dve))
                eng.wait_ge(S.order_dve, p.now(S.order_dve))
            eng.memset(MV[:, :, :, P:VW], 1.0).then_inc(S.order_dve, p.inc(S.order_dve))
            eng.wait_ge(S.order_dve, p.now(S.order_dve))
            eng.wait_ge(S.gate_in, p.next(S.gate_in))
            for d in range(2):
                R = rows[d]
                ts(GF[R, :], GF[R, :], 0.0, None, ALU.min).then_inc(S.order_dve, p.inc(S.order_dve))
                eng.wait_ge(S.order_dve, p.now(S.order_dve))
                tt(GF[R, :], GF[R, :], GT_[R, :], ALU.subtract).then_inc(S.order_dve, p.inc(S.order_dve))
                eng.wait_ge(S.order_dve, p.now(S.order_dve))
                for lo in (0, SEQ):
                    hi = lo + SEQ
                    s_ = slice(lo, hi) if d == 0 else slice(hi - 1, lo - 1 if lo else None, -1)
                    scan(GB[R, s_], ones_row[R, 0:SEQ], GF[R, s_], 0.0, ALU.mult, ALU.add).then_inc(S.order_dve, p.inc(S.order_dve))
                    eng.wait_ge(S.order_dve, p.now(S.order_dve))
                tt(GI[R, :], GI[R, :], GB[R, :], ALU.subtract).then_inc(S.order_dve, p.inc(S.order_dve))
                eng.wait_ge(S.order_dve, p.now(S.order_dve))
                eng.tensor_reduce(G1[R, 0:1], GI[R, SEQ:2 * SEQ], AX_X, ALU.max).then_inc(S.order_dve, p.inc(S.order_dve))
                eng.wait_ge(S.order_dve, p.now(S.order_dve))
                ts(G1[R, 0:1], G1[R, 0:1], 0.0, None, ALU.max).then_inc(S.order_dve, p.inc(S.order_dve))
                eng.wait_ge(S.order_dve, p.now(S.order_dve))
                ts(G1[R, 1:2], G1[R, 0:1], -1.0, None, ALU.mult).then_inc(S.order_dve, p.inc(S.order_dve))
                eng.wait_ge(S.order_dve, p.now(S.order_dve))
                end = 2 * SEQ - 1 if d == 0 else SEQ
                tt(G1[R, 2:3], G1[R, 0:1], GB[R, end:end + 1], ALU.add).then_inc(S.order_dve, p.inc(S.order_dve))
                eng.wait_ge(S.order_dve, p.now(S.order_dve))
                s_ = slice(0, SEQ) if d == 0 else slice(SEQ - 1, None, -1)
                scan(GM[R, s_], GI[R, s_], GI[R, s_], G1[R, 2:3], ALU.max, ALU.max).then_inc(S.order_dve, p.inc(S.order_dve))
                eng.wait_ge(S.order_dve, p.now(S.order_dve))
                eng.tensor_copy(G4[R, 0, :], GI[R, 0:SEQ]).then_inc(S.order_dve, p.inc(S.order_dve))
                eng.wait_ge(S.order_dve, p.now(S.order_dve))
                sem = S.gate_m if d else S.order_dve
                tt(GT_[R, 0:SEQ], GB[R, 0:SEQ], GM[R, :], ALU.add).then_inc(sem, p.inc(sem))
                eng.wait_ge(sem, p.now(sem))
            tt(SEL2[0:40, :], ident[0:40, 0:HEADS], ident[0:40, 32:32 + HEADS], ALU.add).then_inc(S.order_dve, p.inc(S.order_dve))
            eng.wait_ge(S.order_dve, p.now(S.order_dve))
            eng.wait_ge(S.gate_exp, p.next(S.gate_exp))
            eng.wait_ge(S.tg_full, p.next(S.tg_full))
            eng.tensor_copy(TG[:, :, :], bank[4][:, 0:320].rearrange("p (a b) -> p a b", a=8)).then_inc(S.order_dve, p.inc(S.order_dve))
            eng.wait_ge(S.order_dve, p.now(S.order_dve))
            eng.memset(tick[:, 0:1], 0.0).then_inc(S.free[4], p.inc(S.free[4]))
            eng.wait_ge(S.free[4], p.now(S.free[4]))
            eng.memset(tick[:, 0:1], 0.0).then_inc(S.tg_ready, p.inc(S.tg_ready))
            eng.wait_ge(S.tg_ready, p.now(S.tg_ready))

            p.meet("memory")
            with p.loop(PAIRS) as i:
                def sel(h):
                    return SEL2[0:40, bass.ds(i * 2 + h, 1)]

                def tg(q, d, h, n=1):
                    return TG[:, q:q + n, bass.ds(i * 2 + (32 * d + h), 1)]

                for h in range(2):
                    ts(MR[0:40, h, 0, :], GM[0:40, :], sel(h), None, ALU.mult)
                    ins = ts(MR[0:40, h, 1, :], G4[0:40, 2, :], sel(h), -1.0, ALU.mult, ALU.mult)
                ins.then_inc(S.mrow, p.inc(S.mrow))
                eng.wait_ge(S.mrow, p.now(S.mrow))
                p.skip(S.done[0])
                eng.wait_ge(S.free[0], p.next(S.free[0]))
                eng.wait_ge(S.free[1], p.next(S.free[1]))
                for d in range(2):
                    w = TG[:, 2:4, bass.ds(i * 2 + 32 * d, 2)].unsqueeze(3).to_broadcast([P, 2, 2, DH])
                    ins = tt(KW[:, 2 * d:2 * d + 2, :, :], MKC[:, :, :].rearrange("p t (h c) -> p t h c", h=2), w, ALU.mult)
                ins.then_inc(S.kw, p.inc(S.kw))
                eng.wait_ge(S.kw, p.now(S.kw))
                p.skip(S.done[1])
                p.skip(S.free[2])
                p.skip(S.free[3])
                for h in range(2):
                    R = slice(DH * h, DH * h + DH)
                    eng.wait_ge(S.wb_full, p.next(S.wb_full))
                    tt(QW[R, h, :, :], MQ[R, :].unsqueeze(1).to_broadcast([DH, 2, SEQ]),
                               bank[h][R, :].rearrange("p (a b) -> p a b", a=2), ALU.mult).then_inc(S.free[h], p.inc(S.free[h]))
                    eng.wait_ge(S.free[h], p.now(S.free[h]))
                p.skip(S.free[7])

                def decay(h):
                    parts = [(0, 0, 0, 2, 0), (0, 1, 2, 1, P), (1, 0, 3, 1, 0), (1, 1, 4, 2, 0)]
                    eng.wait_ge(S.nm_full, p.next(S.nm_full))
                    for d, s_, b0, nb, q0 in parts:
                        ins = ts(flat(EE[:, h, b0:b0 + nb, :]), bank[5][:, d * SEQ + q0:d * SEQ + q0 + nb * P],
                                 flat(tg(s_, d, h)), 0.0, ALU.add, ALU.min)
                    ins.then_inc(S.free[5], p.inc(S.free[5]))
                    eng.wait_ge(S.free[5], p.now(S.free[5]))
                    eng.wait_ge(S.e_exp, p.next(S.e_exp))
                    for d, s_, b0, nb, q0 in parts:
                        ins = tt(flat(EE[:, h, b0:b0 + nb, :]), flat(EE[:, h, b0:b0 + nb, :]),
                                 bank[4][:, s_ * SEQ + q0:s_ * SEQ + q0 + nb * P], ALU.mult)
                    ins.then_inc(S.free[4], p.inc(S.free[4]))
                    eng.wait_ge(S.free[4], p.now(S.free[4]))
                    for d in range(2):
                        ins = tt(EE[:, h, 3 * d:3 * d + 3:2, :], EE[:, h, 3 * d:3 * d + 3:2, :],
                                 tri[:, d, :].unsqueeze(1).to_broadcast([P, 2, P]), ALU.mult)
                    ins.then_inc(S.e_ready, p.inc(S.e_ready))
                    eng.wait_ge(S.e_ready, p.now(S.e_ready))

                def combine(h):
                    eng.wait_ge(S.num_full, p.next(S.num_full))
                    for d in range(2):
                        den = bank[6 + d][:, 0:2 * VW].rearrange("p (a b) -> p a b", a=2)[:, :, P]
                        dn = DN[:, h, 2 * d:2 * d + 2]
                        ts(dn, den, -1.0, None, ALU.mult).then_inc(S.order_dve, p.inc(S.order_dve))
                        eng.wait_ge(S.order_dve, p.now(S.order_dve))
                        tt(dn, dn, den, ALU.max).then_inc(S.order_dve, p.inc(S.order_dve))
                        eng.wait_ge(S.order_dve, p.now(S.order_dve))
                        tt(dn, dn, flat(tg(6, d, h, 2)), ALU.max).then_inc(S.order_dve, p.inc(S.order_dve))
                        eng.wait_ge(S.order_dve, p.now(S.order_dve))
                    eng.reciprocal(RD[:, h, :], DN[:, h, :]).then_inc(S.order_dve, p.inc(S.order_dve))
                    eng.wait_ge(S.order_dve, p.now(S.order_dve))
                    for t in range(2):
                        ins = ts(HS[:, h, t, :], bank[6][:, t * VW:t * VW + P], RD[:, h, t:t + 1], None, ALU.mult)
                    ins.then_inc(S.free[6], p.inc(S.free[6]))
                    eng.wait_ge(S.free[6], p.now(S.free[6]))
                    for t in range(2):
                        ins = stt(HS[:, h, t, :], bank[7][:, t * VW:t * VW + P], RD[:, h, 2 + t:3 + t], HS[:, h, t, :],
                                  ALU.mult, ALU.add)
                    ins.then_inc(S.free[7], p.inc(S.free[7]))
                    eng.wait_ge(S.free[7], p.now(S.free[7]))
                    eng.memset(DN[:, h, 0:1], 0.0).then_inc(S.hs, p.inc(S.hs))
                    eng.wait_ge(S.hs, p.now(S.hs))
                    eng.wait_ge(S.mrs, p.next(S.mrs))
                    for t in range(2):
                        ins = stt(HM[:, h, t, :], HS[:, h, t, :], RR[:, h, t:t + 1], MO[:, t, h * P:(h + 1) * P], ALU.mult, ALU.mult)
                    ins.then_inc(S.hm, p.inc(S.hm))
                    eng.wait_ge(S.hm, p.now(S.hm))

                decay(0)
                p.skip(S.done[2])
                eng.wait_ge(S.free[0], p.next(S.free[0]))
                eng.wait_ge(S.free[1], p.next(S.free[1]))
                decay(1)
                combine(0)
                combine(1)
                p.skip(S.half[3])
                p.skip(S.done[3])
                p.skip(S.free[2])
                p.skip(S.free[3])
                p.skip(S.free[0])

            for v in (*QL, *KL):
                eng.memset(v[:, :, :], 0.0).then_inc(S.order_dve, p.inc(S.order_dve))
                eng.wait_ge(S.order_dve, p.now(S.order_dve))
            p.meet("recurrence")
            with p.loop(PAIRS) as i:
                for r in (0,):
                    p.skip(S.half[r])
                    p.skip(S.done[r])
                eng.wait_ge(S.free[0], p.next(S.free[0]))
                eng.wait_ge(S.free[1], p.next(S.free[1]))

                def unit(d):
                    r, b0 = ((1, 2), (2, 0))[d]
                    p.skip(S.half[r])
                    p.skip(S.done[r])
                    for t in range(2):
                        eng.wait_ge(S.free[b0 + t], p.next(S.free[b0 + t]))
                        c = i * 2 + (8 * d + t)
                        ts(FF_[:, d, t, :], FF_[:, d, t, :], LBC[:, 1, bass.ds(c, 1)], LBC[:, 0, bass.ds(c, 1)], ALU.mult, ALU.add)
                        ins = ts(KK[:, d, t, :], KK[:, d, t, :], LBC[:, 1, bass.ds(c, 1)], None, ALU.mult)
                    ins.then_inc(S.kk, p.inc(S.kk))
                    eng.wait_ge(S.kk, p.now(S.kk))
                    eng.memset(SUF[:, :, :], 1.0).then_inc(S.order_dve, p.inc(S.order_dve))
                    eng.wait_ge(S.order_dve, p.now(S.order_dve))
                    F = FF_[:, d, :, 0:SEQ]
                    K = KK[:, d, :, 0:SEQ]

                    def halves(v, h):
                        v = v.rearrange("p a (n j) -> p a n j", j=2 * h)
                        return (v[:, :, :, 0:h], v[:, :, :, h:2 * h])

                    def edge(h, j):
                        v = F.rearrange("p a (n j) -> p a n j", j=2 * h)[:, :, :, j:j + 1]
                        return v.to_broadcast([P, 2, SEQ // (2 * h), h])

                    kh, qh = (0, 1) if d == 0 else (1, 0)

                    def products(lev):
                        h = 1 << lev
                        tt(halves(QL[lev % 2][:, :, :], h)[qh], halves(HQ[:, :, :], h)[qh], halves(F, h)[qh], ALU.mult)
                        tt(halves(KL[lev % 2][:, :, :], h)[kh], halves(K, h)[kh], halves(SUF[:, :, :], h)[kh], ALU.mult).then_inc(S.lev_ready, p.inc(S.lev_ready))
                        eng.wait_ge(S.lev_ready, p.now(S.lev_ready))
                        s_, f = halves(SUF[:, :, :], h)[kh], halves(F, h)[qh]
                        if lev < 7:
                            tt(s_, s_, edge(h, 2 * h - 1 if d == 0 else 0), ALU.mult).then_inc(S.order_dve, p.inc(S.order_dve))
                            eng.wait_ge(S.order_dve, p.now(S.order_dve))
                        tt(f, f, edge(h, h - 1 if d == 0 else h), ALU.mult).then_inc(S.order_dve, p.inc(S.order_dve))
                        eng.wait_ge(S.order_dve, p.now(S.order_dve))

                    def pick(lev):
                        b = 4 + (lev + 1) % 2
                        eng.wait_ge(S.lev_full, p.next(S.lev_full))
                        p.fence()
                        m = lmask[:, lev, d, :].unsqueeze(1).to_broadcast([P, 4, P])
                        eng.copy_predicated(AT[:, d, :, :], m, bank[b][:, :].rearrange("p (a b) -> p a b", a=4)).then_inc(S.free[b], p.inc(S.free[b]))
                        eng.wait_ge(S.free[b], p.now(S.free[b]))

                    products(0)
                    eng.wait_ge(S.lev_full, p.next(S.lev_full))
                    tt(AT[:, d, :, :], bank[4][:, :].rearrange("p (a b) -> p a b", a=4),
                               ident[:, :].unsqueeze(1).to_broadcast([P, 4, P]), ALU.mult).then_inc(S.free[4], p.inc(S.free[4]))
                    eng.wait_ge(S.free[4], p.now(S.free[4]))
                    for lev in range(7):
                        products(lev + 1)
                        pick(lev)
                    eng.memset(tick[:, 0:1], 0.0).then_inc(S.at, p.inc(S.at))
                    eng.wait_ge(S.at, p.now(S.at))
                    p.skip(S.lev_full)
                    p.skip(S.free[4])
                    tt(QR[:, d, :, :], HQ[:, :, :], F, ALU.mult).then_inc(S.inter, p.inc(S.inter))
                    eng.wait_ge(S.inter, p.now(S.inter))
                    if d == 1:
                        eng.wait_ge(S.kct_full, p.next(S.kct_full))
                    for t in range(2):
                        if d == 0:
                            eng.memset(SUFC[:, t, SEQ - 1:SEQ], 1.0)
                            scan(SUFC[:, t, SEQ - 2::-1] if SEQ - 2 >= 0 else None, FF_[:, d, t, 2 * SEQ - 1:SEQ:-1],
                                      ones_row[:, 0:SEQ - 1], 1.0, ALU.mult, ALU.mult).then_inc(S.order_dve, p.inc(S.order_dve))
                            eng.wait_ge(S.order_dve, p.now(S.order_dve))
                        else:
                            eng.memset(SUFC[:, t, 0:1], 1.0)
                            scan(SUFC[:, t, 1:SEQ], FF_[:, d, t, SEQ:2 * SEQ - 1], ones_row[:, 0:SEQ - 1], 1.0,
                                      ALU.mult, ALU.mult).then_inc(S.order_dve, p.inc(S.order_dve))
                            eng.wait_ge(S.order_dve, p.now(S.order_dve))
                    tt(KC[:, :, :], KK[:, d, :, SEQ:2 * SEQ], SUFC[:, :, :], ALU.mult).then_inc(S.kc, p.inc(S.kc))
                    eng.wait_ge(S.kc, p.now(S.kc))
                    p.skip(S.free[7])

                unit(0)
                unit(1)
                p.skip(S.kct_full)
                p.skip(S.done[3])
                p.skip(S.free[2])
                p.skip(S.free[3])
                p.skip(S.free[7], 3)
                eng.wait_ge(S.ors, p.next(S.ors))
                for h in range(2):
                    hs = slice(h * SEQ, (h + 1) * SEQ)
                    ins = stt(OT[:, hs], bank[6][:, hs], P2[:, bass.ds(i * 2 + (B_HG + h), 1)], RS[:, hs], ALU.mult, ALU.mult)
                ins.then_inc(S.free[6], p.inc(S.free[6]))
                eng.wait_ge(S.free[6], p.now(S.free[6]))
                for h in range(2):
                    hs = slice(h * SEQ, (h + 1) * SEQ)
                    o = flat(HHT[:, bass.ds(i * 2 + h, 1), :]).rearrange("p (r c) -> p c r", r=4)
                    g = flat(HG[:, bass.ds(i * 2 + h, 1), :])
                    ins = tt(o, OT[:, hs].rearrange("p (c r) -> p c r", r=4), g.rearrange("p (c r) -> p c r", r=4), ALU.mult)
                ins.then_inc(S.hhd, p.inc(S.hhd))
                eng.wait_ge(S.hhd, p.now(S.hhd))

            gms, ghs = HQ, HI[:, 0:2, :]
            p.meet("merge")
            with p.loop(PAIRS) as i:
                for r in (0, 1):
                    p.skip(S.half[r])
                    p.skip(S.done[r])
                for b in range(4):
                    eng.wait_ge(S.free[b], p.next(S.free[b]))
                for r, gate, dst in ((2, gms, SUF), (3, ghs, SUFC)):
                    for t in range(2):
                        sem = S.done[r] if t else S.half[r]
                        eng.wait_ge(sem, p.next(sem))
                        b = 2 * (r % 2) + t
                        tt(dst[:, t, :], gate[:, t, :], bank[b][:, 0:SEQ], ALU.mult).then_inc(S.free[b], p.inc(S.free[b]))
                        eng.wait_ge(S.free[b], p.now(S.free[b]))
                tt(MRG[:, bass.ds(i * 2, 2), :], SUF[:, :, :], SUFC[:, :, :], ALU.add).then_inc(S.mrg, p.inc(S.mrg))
                eng.wait_ge(S.mrg, p.now(S.mrg))
                eng.memset(tick[:, 0:1], 0.0).then_inc(S.mrg, p.inc(S.mrg))
                eng.wait_ge(S.mrg, p.now(S.mrg))
            p.meet("output")
            for r in range(4):
                for t in range(2):
                    sem = S.done[r] if t else S.half[r]
                    eng.wait_ge(sem, p.next(sem))
                    b = 2 * (r % 2) + t
                    m = 2 * r + t
                    stt(H2[:, m, 0:SEQ], bank[b][:, 0:SEQ], GATE[:, 1, m, 0:1], H2[:, m, 0:SEQ], ALU.mult, ALU.add).then_inc(S.free[b], p.inc(S.free[b]))
                    eng.wait_ge(S.free[b], p.now(S.free[b]))
            eng.memset(tick[:, 0:1], 0.0).then_inc(S.x2_ready, p.inc(S.x2_ready))
            eng.wait_ge(S.x2_ready, p.now(S.x2_ready))
            p.meet("feed")
            ffn(SEQ, 0, 2)
            eng.wait_ge(S.rs, p.next(S.rs))
            p.skip(S.free[4])
            for k in range(KD):
                stt(U[:, k, 0:SEQ], H2[:, k, 0:SEQ], P2[:, B_FIN + k:B_FIN + k + 1], RS[:, 0:SEQ], ALU.mult, ALU.mult).then_inc(S.u, p.inc(S.u))
            for t in range(2):
                for half in range(2):
                    b = 4 + 2 * t + half
                    eng.wait_ge(S.tr_full, p.next(S.tr_full))
                    eng.tensor_copy(XT[:, t, half * 512:(half + 1) * 512], bank[b][:, :]).then_inc(S.order_dve, p.inc(S.order_dve))
                    eng.wait_ge(S.order_dve, p.now(S.order_dve))
                eng.memset(tick[:, 0:1], 0.0).then_inc(S.out_ready, p.inc(S.out_ready))
                eng.wait_ge(S.out_ready, p.now(S.out_ready))


_INS = ['x', 'meta_tokens', 'mix_pre_g', 'mix_post_g', 'w_in', 'b_forget', 'a_dw_w', 'a_dw_b', 'a_ln_g', 'a_ln_b',
        'a_pw_w', 'sc_conv_w', 'head_g', 'w_out', 'ffn_pre_g', 'ffn_post_g', 'ffn_w_up', 'ffn_conv_w', 'ffn_w_down',
        'c_2', 'ctx_2', 'c_ctx_2', 'ada_w_2', 'ada_b_2', 'ffn1_norm_2', 'ffn1_w_in_2', 'ffn1_w_out_2', 'mix_norm_2',
        'mix_w_in_2', 'mix_b_in_2', 'mlstm_norm_2', 'hgrn_lb_logits_2', 'hgrn_norm_2', 'proj_m_2', 'proj_h_2',
        'mix_w_out_2', 'ffn2_norm_2', 'ffn2_w_in_2', 'ffn2_w_out_2', 'final_norm_2']


def build(nc, shapes, rises):
    from concourse import mybir as _mybir
    a = {n: nc.dram_tensor(f"in_{n}_dram", s, _mybir.dt.from_np(t), kind="ExternalInput").ap() for n, (s, t) in shapes.items()}
    out = nc.dram_tensor("out_0_dram", (1, SEQ, D), F32, kind="ExternalOutput").ap()
    first_and_second_block(nc, rises, a, out)


def kernel(**inputs):
    import numpy as _np
    import concourse.bacc as _bacc
    from concourse.bass_utils import run_bass_kernel_spmd as _run

    given = {n: _np.ascontiguousarray(inputs[n]) for n in _INS}
    shapes = {n: (v.shape, v.dtype) for n, v in given.items()}
    rises = {}
    build(_bacc.Bacc("TRN2", target_bir_lowering=False, num_devices=1), shapes, rises)
    nc = _bacc.Bacc("TRN2", target_bir_lowering=False, num_devices=1)
    build(nc, shapes, rises)
    r = _run(nc, [{f"in_{n}_dram": v for n, v in given.items()}], core_ids=[0])
    return r.results[0]["out_0_dram"]
```
